# Optimizing a Trainium2 kernel written in Bass

```python
import math
import jax, jax.numpy as jnp
from jax import lax
import numpy as np
import jax
import jax.numpy as jnp

D_MODEL = 1024
BATCH = 1
SEQ = 256
DEPTH = 2

CHUNK = 64
Q_BLOCK = 128
N_MIXERS = 2
N_RET_LAYERS = (DEPTH + 1) // 2
N_DIFF_LAYERS = DEPTH // 2
MIX_WIDTH = D_MODEL
MEM_LEN = 256
MEM_HEADS = 4
MEM_HEAD_DIM = 64
MEM_WIDTH = MEM_HEADS * MEM_HEAD_DIM
MAIN_WIDTH = MIX_WIDTH - MEM_WIDTH
RET_HEADS = 6
RET_V_DIM = MAIN_WIDTH // RET_HEADS
RET_QK_DIM = RET_V_DIM // 2
DIFF_HEADS = 6
DIFF_HEAD_DIM = MAIN_WIDTH // (2 * DIFF_HEADS)
DIFF_V_DIM = 2 * DIFF_HEAD_DIM
IN_WIDTH = 3 * MAIN_WIDTH + MEM_WIDTH
FFN_DIM = -(-8 * D_MODEL // (3 * 256)) * 256
EPS = 1e-6


def rms_norm(x, w):
    x32 = x.astype(jnp.float32)
    y = x32 * lax.rsqrt(jnp.mean(x32 * x32, axis=-1, keepdims=True) + EPS)
    return (y * w.astype(jnp.float32)).astype(x.dtype)

def retention(q, k, v):
    B, S, H, dk = q.shape
    dv = v.shape[-1]
    nc = S // CHUNK
    dt = q.dtype
    log_gamma = jnp.log(1.0 - 2.0 ** (-5.0 - jnp.arange(H, dtype=jnp.float32)))
    k = k * (dk ** -0.5)
    q = q.reshape(B, nc, CHUNK, H, dk)
    k = k.reshape(B, nc, CHUNK, H, dk)
    v = v.reshape(B, nc, CHUNK, H, dv)
    pos = jnp.arange(CHUNK, dtype=jnp.float32)
    d_in = jnp.exp(log_gamma[:, None, None] * jnp.abs(pos[:, None] - pos[None, :])).astype(dt)
    s_in = jnp.einsum('bnihd,bnjhd->bnhij', q, k) * d_in
    o_in = jnp.einsum('bnhij,bnjhe->bnihe', s_in, v)
    k_dec = jnp.exp(log_gamma[:, None] * (CHUNK - 1 - pos)[None, :]).astype(dt)
    kv = jnp.einsum('bnjhd,hj,bnjhe->bnhde', k, k_dec, v)
    chunk_dec = jnp.exp(log_gamma * CHUNK).astype(dt)[:, None, None]

    def step(state, kv_c):
        return state * chunk_dec + kv_c, state

    init = jnp.zeros((B, H, dk, dv), dtype=kv.dtype)
    _, prev = lax.scan(step, init, jnp.moveaxis(kv, 1, 0))
    prev = jnp.moveaxis(prev, 0, 1)
    q_dec = jnp.exp(log_gamma[:, None] * (pos + 1.0)[None, :]).astype(dt)
    o_x = jnp.einsum('bnihd,hi,bnhde->bnihe', q, q_dec, prev)
    return (o_in + o_x).reshape(B, S, H, dv)

def diff_attention(q, k, v, lam):
    B, S, H, _, d = q.shape
    nb = S // Q_BLOCK
    slopes = 2.0 ** (-8.0 * jnp.arange(1, H + 1, dtype=jnp.float32) / H)
    s_pos = jnp.arange(S)
    s_chunk = s_pos // CHUNK
    qb = jnp.moveaxis(q.reshape(B, nb, Q_BLOCK, H, 2, d), 1, 0)
    starts = jnp.arange(nb, dtype=jnp.int32) * Q_BLOCK
    scale = d ** -0.5

    def block(args):
        qblk, t0 = args
        t = t0 + jnp.arange(Q_BLOCK)
        sc = jnp.einsum('bihcd,bjhcd->bhcij', qblk, k).astype(jnp.float32) * scale
        dist = jnp.abs(t[:, None] - s_pos[None, :]).astype(jnp.float32)
        bias = -slopes[:, None, None] * dist[None]
        allowed = s_chunk[None, :] <= (t // CHUNK)[:, None]
        sc = jnp.where(allowed, sc + bias[None, :, None], -jnp.inf)
        p = jax.nn.softmax(sc, axis=-1)
        a = p[:, :, 0] - lam * p[:, :, 1]
        return jnp.einsum('bhij,bjhe->bihe', a.astype(v.dtype), v)

    o = lax.map(block, (qb, starts))
    return jnp.moveaxis(o, 0, 1).reshape(B, S, H, v.shape[-1])

def memory_attention(qc, mk, mv):
    sc = jnp.einsum('bshd,bmhd->bhsm', qc, mk).astype(jnp.float32) * (qc.shape[-1] ** -0.5)
    p = jax.nn.softmax(sc, axis=-1).astype(mv.dtype)
    return jnp.einsum('bhsm,bmhd->bshd', p, mv)

def first_inputs(seed: int = 0) -> dict:
    key = jax.random.key(seed)
    ks = jax.random.split(key, 24)
    n = jax.random.normal
    f = jnp.float32

    def gain(k, shape):
        return 1.0 + 0.02 * n(k, shape, f)

    return {
        'x': n(ks[0], (BATCH, SEQ, D_MODEL), f),
        'mem': n(ks[1], (BATCH, MEM_LEN, D_MODEL), f),
        'attn_norm_w': gain(ks[2], (DEPTH, D_MODEL)),
        'w_in': n(ks[3], (DEPTH, D_MODEL, IN_WIDTH), f) * D_MODEL ** -0.5,
        'w_out': n(ks[4], (DEPTH, MIX_WIDTH, D_MODEL), f) * MIX_WIDTH ** -0.5,
        'mem_norm_w': gain(ks[5], (D_MODEL,)),
        'w_mem_kv': n(ks[6], (DEPTH, D_MODEL, 2 * MEM_WIDTH), f) * D_MODEL ** -0.5,
        'mem_q_norm_w': gain(ks[7], (DEPTH, MEM_HEAD_DIM)),
        'mem_k_norm_w': gain(ks[8], (DEPTH, MEM_HEAD_DIM)),
        'ret_gn_w': gain(ks[9], (N_RET_LAYERS, RET_HEADS, RET_V_DIM)),
        'diff_q_norm_w': gain(ks[10], (N_DIFF_LAYERS, DIFF_HEAD_DIM)),
        'diff_k_norm_w': gain(ks[11], (N_DIFF_LAYERS, DIFF_HEAD_DIM)),
        'diff_lambda_q1': 0.1 * n(ks[12], (N_DIFF_LAYERS, DIFF_HEAD_DIM), f),
        'diff_lambda_k1': 0.1 * n(ks[13], (N_DIFF_LAYERS, DIFF_HEAD_DIM), f),
        'diff_lambda_q2': 0.1 * n(ks[14], (N_DIFF_LAYERS, DIFF_HEAD_DIM), f),
        'diff_lambda_k2': 0.1 * n(ks[15], (N_DIFF_LAYERS, DIFF_HEAD_DIM), f),
        'diff_subln_w': gain(ks[16], (N_DIFF_LAYERS, DIFF_V_DIM)),
        'ffn_norm_w': gain(ks[17], (DEPTH, D_MODEL)),
        'w_gate_up': n(ks[18], (DEPTH, D_MODEL, 2 * FFN_DIM), f) * D_MODEL ** -0.5,
        'w_down': n(ks[19], (DEPTH, FFN_DIM, D_MODEL), f) * FFN_DIM ** -0.5,
    }

def first_block(x, mem, attn_norm_w, w_in, w_out, mem_norm_w, w_mem_kv, mem_q_norm_w,
              mem_k_norm_w, ret_gn_w, diff_q_norm_w, diff_k_norm_w, diff_lambda_q1,
              diff_lambda_k1, diff_lambda_q2, diff_lambda_k2, diff_subln_w, ffn_norm_w,
              w_gate_up, w_down):
    B, S, _ = x.shape
    M = mem.shape[1]
    memn = rms_norm(mem, mem_norm_w)
    for layer in range(DEPTH):
        h = rms_norm(x, attn_norm_w[layer])
        u = h @ w_in[layer]
        j = layer // N_MIXERS
        if layer % N_MIXERS == 0:
            nqk = RET_HEADS * RET_QK_DIM
            q = u[..., :nqk].reshape(B, S, RET_HEADS, RET_QK_DIM)
            k = u[..., nqk:2 * nqk].reshape(B, S, RET_HEADS, RET_QK_DIM)
            v = u[..., 2 * nqk:2 * nqk + MAIN_WIDTH].reshape(B, S, RET_HEADS, RET_V_DIM)
            g = u[..., 2 * nqk + MAIN_WIDTH:3 * MAIN_WIDTH]
            o = rms_norm(retention(q, k, v), ret_gn_w[j])
            o_main = jax.nn.silu(g) * o.reshape(B, S, MAIN_WIDTH)
        else:
            q = u[..., :MAIN_WIDTH].reshape(B, S, DIFF_HEADS, 2, DIFF_HEAD_DIM)
            k = u[..., MAIN_WIDTH:2 * MAIN_WIDTH].reshape(B, S, DIFF_HEADS, 2, DIFF_HEAD_DIM)
            v = u[..., 2 * MAIN_WIDTH:3 * MAIN_WIDTH].reshape(B, S, DIFF_HEADS, DIFF_V_DIM)
            q = rms_norm(q, diff_q_norm_w[j])
            k = rms_norm(k, diff_k_norm_w[j])
            lambda_init = 0.8 - 0.6 * math.exp(-0.3 * layer)
            lq1 = diff_lambda_q1[j].astype(jnp.float32)
            lk1 = diff_lambda_k1[j].astype(jnp.float32)
            lq2 = diff_lambda_q2[j].astype(jnp.float32)
            lk2 = diff_lambda_k2[j].astype(jnp.float32)
            lam = jnp.exp(jnp.sum(lq1 * lk1)) - jnp.exp(jnp.sum(lq2 * lk2)) + lambda_init
            o = rms_norm(diff_attention(q, k, v, lam), diff_subln_w[j]) * (1.0 - lambda_init)
            o_main = o.reshape(B, S, MAIN_WIDTH)
        qc = rms_norm(u[..., 3 * MAIN_WIDTH:].reshape(B, S, MEM_HEADS, MEM_HEAD_DIM), mem_q_norm_w[layer])
        mkv = memn @ w_mem_kv[layer]
        mk = rms_norm(mkv[..., :MEM_WIDTH].reshape(B, M, MEM_HEADS, MEM_HEAD_DIM), mem_k_norm_w[layer])
        mv = mkv[..., MEM_WIDTH:].reshape(B, M, MEM_HEADS, MEM_HEAD_DIM)
        o_mem = memory_attention(qc, mk, mv).reshape(B, S, MEM_WIDTH)
        x = x + jnp.concatenate([o_main, o_mem], axis=-1) @ w_out[layer]
        h = rms_norm(x, ffn_norm_w[layer])
        gu = h @ w_gate_up[layer]
        x = x + (jax.nn.silu(gu[..., :FFN_DIM]) * gu[..., FFN_DIM:]) @ w_down[layer]
    return x


DEPTH_2 = 1

HEAD_DIM = 64
SSD_HEADS = 16
SSD_GROUPS = 2
SSD_STATE = 128
SSD_CONV = 4
SSD_CHUNK = 128
SSD_WIDTH = SSD_HEADS * HEAD_DIM
SSD_BC_WIDTH = SSD_GROUPS * SSD_STATE
SSD_XBC_WIDTH = SSD_WIDTH + 2 * SSD_BC_WIDTH
FOX_HEADS = 16
FOX_WIDTH = FOX_HEADS * HEAD_DIM
MIX_WIDTH_2 = SSD_WIDTH + FOX_WIDTH
D_FF = 2816
FFN_CONV = 3
NORM_EPS = 1e-6
Z_END = SSD_WIDTH
XBC_END = Z_END + SSD_XBC_WIDTH
DT_END = XBC_END + SSD_HEADS
Q_END = DT_END + FOX_WIDTH
K_END = Q_END + FOX_WIDTH
V_END = K_END + FOX_WIDTH
IN_COLS = V_END + FOX_HEADS


def rms_norm_2(x, w):
    xf = x.astype(jnp.float32)
    y = xf * lax.rsqrt(jnp.mean(xf * xf, axis=-1, keepdims=True) + NORM_EPS)
    return (y * w.astype(jnp.float32)).astype(x.dtype)

def causal_depthwise_conv(x, w, b):
    k = w.shape[0]
    y = lax.conv_general_dilated(
        x, w[:, None, :].astype(x.dtype), window_strides=(1,), padding=[(k - 1, 0)],
        dimension_numbers=('NWC', 'WIO', 'NWC'), feature_group_count=x.shape[-1])
    return y + b.astype(x.dtype)

def ssd_mixer(xbc_raw, z, dt_raw, conv_w, conv_b, dt_bias, a_log, d_skip, norm_w):
    b, s, _ = xbc_raw.shape
    nc = s // SSD_CHUNK
    e = SSD_HEADS // SSD_GROUPS
    xbc = jax.nn.silu(causal_depthwise_conv(xbc_raw, conv_w, conv_b))
    xs, bm, cm = jnp.split(xbc, [SSD_WIDTH, SSD_WIDTH + SSD_BC_WIDTH], axis=-1)
    x6 = xs.reshape(b, nc, SSD_CHUNK, SSD_GROUPS, e, HEAD_DIM)
    bm = bm.reshape(b, nc, SSD_CHUNK, SSD_GROUPS, SSD_STATE)
    cm = cm.reshape(b, nc, SSD_CHUNK, SSD_GROUPS, SSD_STATE)
    dt = jax.nn.softplus(dt_raw.astype(jnp.float32) + dt_bias.astype(jnp.float32))
    a = -jnp.exp(a_log.astype(jnp.float32))
    dt5 = dt.reshape(b, nc, SSD_CHUNK, SSD_GROUPS, e)
    a_cs = jnp.cumsum(dt5 * a.reshape(SSD_GROUPS, e), axis=2)
    xdt = x6 * dt5[..., None]
    at = jnp.moveaxis(a_cs, 2, -1)
    seg = at[..., :, None] - at[..., None, :]
    tri = jnp.tril(jnp.ones((SSD_CHUNK, SSD_CHUNK), dtype=bool))
    decay = jnp.exp(jnp.where(tri, seg, -jnp.inf))
    cb = jnp.einsum('bclgn,bcsgn->bcgls', cm, bm)
    scores = cb[:, :, :, None] * decay
    y_diag = jnp.einsum('bcgels,bcsgep->bclgep', scores, xdt)
    decay_to_end = jnp.exp(a_cs[:, :, -1:] - a_cs)
    chunk_states = jnp.einsum('bclgn,bclgep->bcgepn', bm, xdt * decay_to_end[..., None])
    chunk_decay = jnp.exp(a_cs[:, :, -1])

    def step(h, inp):
        dec, st = inp
        return h * dec[..., None, None] + st, h

    h0 = jnp.zeros((b, SSD_GROUPS, e, HEAD_DIM, SSD_STATE), jnp.float32)
    _, states_in = lax.scan(step, h0, (jnp.moveaxis(chunk_decay, 1, 0), jnp.moveaxis(chunk_states, 1, 0)))
    states_in = jnp.moveaxis(states_in, 0, 1)
    y_off = jnp.einsum('bclgn,bcgepn->bclgep', cm, states_in) * jnp.exp(a_cs)[..., None]
    y = y_diag + y_off + d_skip.astype(jnp.float32).reshape(SSD_GROUPS, e)[:, :, None] * x6
    y = y.reshape(b, s, SSD_WIDTH)
    yg = (y * jax.nn.silu(z.astype(jnp.float32))).reshape(b, s, SSD_GROUPS, SSD_WIDTH // SSD_GROUPS)
    yg = yg * lax.rsqrt(jnp.mean(yg * yg, axis=-1, keepdims=True) + NORM_EPS)
    return (yg.reshape(b, s, SSD_WIDTH) * norm_w.astype(jnp.float32)).astype(xbc_raw.dtype)

def fox_mixer(q, k, v, f_raw, f_bias, q_norm_w, k_norm_w):
    b, s, _ = q.shape

    def heads(t):
        return t.reshape(b, s, FOX_HEADS, HEAD_DIM).transpose(0, 2, 1, 3)

    qh = rms_norm_2(heads(q), q_norm_w)
    kh = rms_norm_2(heads(k), k_norm_w)
    vh = heads(v)
    log_f = jax.nn.log_sigmoid(f_raw.astype(jnp.float32) + f_bias.astype(jnp.float32))
    cum = jnp.cumsum(log_f, axis=1).transpose(0, 2, 1)
    scale = HEAD_DIM ** -0.5
    outs = []
    for start in range(0, s, Q_BLOCK):
        end = start + Q_BLOCK
        logits = jnp.einsum('bhqd,bhkd->bhqk', qh[:, :, start:end], kh[:, :, :end],
                            preferred_element_type=jnp.float32) * scale
        logits = logits + cum[:, :, start:end, None] - cum[:, :, None, :end]
        causal = (start + jnp.arange(Q_BLOCK))[:, None] >= jnp.arange(end)[None, :]
        p = jax.nn.softmax(jnp.where(causal, logits, -jnp.inf), axis=-1)
        outs.append(jnp.einsum('bhqk,bhkd->bhqd', p.astype(vh.dtype), vh[:, :, :end]))
    o = jnp.concatenate(outs, axis=2)
    return o.transpose(0, 2, 1, 3).reshape(b, s, FOX_WIDTH)

def conv_gated_mlp(x, w_up, conv_w, conv_b, w_down):
    h = x @ w_up.astype(x.dtype)
    h = causal_depthwise_conv(h, conv_w, conv_b)
    gate, val = jnp.split(h, 2, axis=-1)
    return (jax.nn.silu(gate) * val) @ w_down.astype(x.dtype)

def second_inputs(seed: int = 0) -> dict:
    key = jax.random.key(seed)
    ks = jax.random.split(key, 20)
    L = DEPTH_2

    def nrm(k, shape, scale):
        return jax.random.normal(k, shape, jnp.float32) * scale

    def gain(k, n):
        return 1.0 + 0.02 * jax.random.normal(k, (L, n), jnp.float32)

    dt = jnp.exp(jax.random.uniform(ks[5], (L, SSD_HEADS), jnp.float32, math.log(1e-3), math.log(1e-1)))
    dt_bias = dt + jnp.log(-jnp.expm1(-dt))
    return {
        'x': nrm(ks[0], (BATCH, SEQ, D_MODEL), 1.0),
        'norm_mix_w': gain(ks[1], D_MODEL),
        'w_in': nrm(ks[2], (L, D_MODEL, IN_COLS), D_MODEL ** -0.5),
        'ssd_conv_w': nrm(ks[3], (L, SSD_CONV, SSD_XBC_WIDTH), SSD_CONV ** -0.5),
        'ssd_conv_b': nrm(ks[4], (L, SSD_XBC_WIDTH), 0.02),
        'ssd_dt_bias': dt_bias,
        'ssd_a_log': jnp.log(jax.random.uniform(ks[6], (L, SSD_HEADS), jnp.float32, 1.0, 16.0)),
        'ssd_d': 1.0 + 0.1 * jax.random.normal(ks[7], (L, SSD_HEADS), jnp.float32),
        'ssd_norm_w': gain(ks[8], SSD_WIDTH),
        'fox_f_bias': jax.random.uniform(ks[9], (L, FOX_HEADS), jnp.float32, 2.0, 5.0),
        'fox_q_norm_w': gain(ks[10], HEAD_DIM),
        'fox_k_norm_w': gain(ks[11], HEAD_DIM),
        'w_out': nrm(ks[12], (L, MIX_WIDTH_2, D_MODEL), MIX_WIDTH_2 ** -0.5),
        'norm_ffn_w': gain(ks[13], D_MODEL),
        'w_up': nrm(ks[14], (L, D_MODEL, 2 * D_FF), D_MODEL ** -0.5),
        'ffn_conv_w': nrm(ks[15], (L, FFN_CONV, 2 * D_FF), FFN_CONV ** -0.5),
        'ffn_conv_b': nrm(ks[16], (L, 2 * D_FF), 0.02),
        'w_down': nrm(ks[17], (L, D_FF, D_MODEL), D_FF ** -0.5),
    }

def second_block(x, norm_mix_w, w_in, ssd_conv_w, ssd_conv_b, ssd_dt_bias, ssd_a_log, ssd_d,
              ssd_norm_w, fox_f_bias, fox_q_norm_w, fox_k_norm_w, w_out, norm_ffn_w,
              w_up, ffn_conv_w, ffn_conv_b, w_down):
    for layer in range(DEPTH_2):
        h = rms_norm_2(x, norm_mix_w[layer])
        proj = h @ w_in[layer].astype(h.dtype)
        z, xbc, dt_raw, q, k, v, f_raw = jnp.split(
            proj, [Z_END, XBC_END, DT_END, Q_END, K_END, V_END], axis=-1)
        y_ssd = ssd_mixer(xbc, z, dt_raw, ssd_conv_w[layer], ssd_conv_b[layer], ssd_dt_bias[layer],
                          ssd_a_log[layer], ssd_d[layer], ssd_norm_w[layer])
        y_fox = fox_mixer(q, k, v, f_raw, fox_f_bias[layer], fox_q_norm_w[layer], fox_k_norm_w[layer])
        mixed = jnp.concatenate([y_ssd, y_fox.astype(y_ssd.dtype)], axis=-1)
        x = x + (mixed @ w_out[layer].astype(mixed.dtype)).astype(x.dtype)
        hf = rms_norm_2(x, norm_ffn_w[layer])
        x = x + conv_gated_mlp(hf, w_up[layer], ffn_conv_w[layer], ffn_conv_b[layer], w_down[layer]).astype(x.dtype)
    return x


def setup_inputs(seed=0):
    out = dict(first_inputs(seed))
    for name, value in second_inputs(seed + 1).items():
        if name != "x":
            out[name + "_2"] = value
    return out


def reference(
    x, mem, attn_norm_w, w_in, w_out, mem_norm_w, w_mem_kv, mem_q_norm_w, mem_k_norm_w,
    ret_gn_w, diff_q_norm_w, diff_k_norm_w, diff_lambda_q1, diff_lambda_k1, diff_lambda_q2,
    diff_lambda_k2, diff_subln_w, ffn_norm_w, w_gate_up, w_down, norm_mix_w_2, w_in_2,
    ssd_conv_w_2, ssd_conv_b_2, ssd_dt_bias_2, ssd_a_log_2, ssd_d_2, ssd_norm_w_2, fox_f_bias_2,
    fox_q_norm_w_2, fox_k_norm_w_2, w_out_2, norm_ffn_w_2, w_up_2, ffn_conv_w_2, ffn_conv_b_2,
    w_down_2,
):
    x = first_block(
        x, mem, attn_norm_w, w_in, w_out, mem_norm_w, w_mem_kv, mem_q_norm_w, mem_k_norm_w,
        ret_gn_w, diff_q_norm_w, diff_k_norm_w, diff_lambda_q1, diff_lambda_k1, diff_lambda_q2,
        diff_lambda_k2, diff_subln_w, ffn_norm_w, w_gate_up, w_down,
    )
    return second_block(
        x, norm_mix_w_2, w_in_2, ssd_conv_w_2, ssd_conv_b_2, ssd_dt_bias_2, ssd_a_log_2,
        ssd_d_2, ssd_norm_w_2, fox_f_bias_2, fox_q_norm_w_2, fox_k_norm_w_2, w_out_2,
        norm_ffn_w_2, w_up_2, ffn_conv_w_2, ffn_conv_b_2, w_down_2,
    )


_drawn_inputs = setup_inputs


def setup_inputs(seed=0):
    import zlib

    import numpy as np

    out = dict(_drawn_inputs(seed))
    spreads = {}
    factors = {'mem_norm_w': 8.0,
     'mem_q_norm_w': 8.0,
     'mem_k_norm_w': 8.0,
     'ret_gn_w': 3.983,
     'diff_q_norm_w': 5.045,
     'diff_k_norm_w': 5.384,
     'diff_lambda_q2': 8.0,
     'diff_subln_w': 5.259,
     'norm_mix_w_2': 4.131,
     'ssd_conv_b_2': 14.709,
     'ssd_norm_w_2': 24.561,
     'fox_q_norm_w_2': 22.566,
     'fox_k_norm_w_2': 8.0,
     'norm_ffn_w_2': 5.796,
     'ffn_conv_b_2': 6.099,
     'ssd_d_2': 64.0}
    for name, (base, spread) in spreads.items():
        noise = np.random.default_rng([zlib.crc32(name.encode()), seed]).standard_normal(out[name].shape)
        drawn = base * np.exp(spread * noise) if base else spread * noise
        out[name] = jnp.asarray(drawn.astype(out[name].dtype))
    for name, factor in factors.items():
        out[name] = (out[name] * factor).astype(out[name].dtype)
    return out
```

```python
import math
from contextlib import ExitStack

import numpy as np

import concourse.bass as bass
from concourse import mybir

P = 128
T = 256
DM = 1024
KT = DM // P
FF = 2816
FT = FF // P
RING = 4
AHEAD = 3
EPS = 1e-6
MASKED = 1e30
LAMBDA_INIT = 0.8 - 0.6 * math.exp(-0.3)
RET_HEADS = DIFF_HEADS = 6
MEM_HEADS = 4
SSD_HEADS = FOX_HEADS = 16

PHASES = [("kv", 8, [8]), ("in0", 20, [8]), ("out0", 8, [8]), ("up0", 44, [8]), ("down0", 24, [8, 8, 6]),
          ("in1", 20, [8]), ("out1", 8, [8]), ("up1", 44, [8]), ("down1", 24, [8, 8, 6]),
          ("in2", 44, [8]), ("dtf", 1, [8]), ("out2", 16, [8, 8]), ("up2", 44, [8]), ("down2", 24, [8, 8, 6])]

PARAMS = [("attn0", 8), ("attn1", 8), ("mem", 8), ("ffn0", 8), ("ffn1", 8), ("mix2", 8), ("ffn2", 8),
          ("memq0", 1), ("memq1", 1), ("memk0", 1), ("memk1", 1), ("gn", 6), ("diffq", 1), ("diffk", 1),
          ("subln", 1), ("lam", 4), ("conv4", 48), ("convb", 12), ("small_b", 1), ("a_log", 1),
          ("skip", 8), ("ssdn", 8), ("foxq", 1), ("foxk", 1), ("conv3", 132), ("conv3b", 44)]
PCOL, _at = {}, 0
for _n, _w in PARAMS:
    PCOL[_n] = _at
    _at += _w
NPARAM = _at

CONSTS = [("ident", 128), ("ones1024", 128), ("ones512", 128), ("ones128", 128), ("ones64", 128),
          ("dist", 384), ("distT", 384), ("causal", 384), ("causalT", 384), ("eps", 8)]
CCOL, _at = {}, 0
for _n, _w in CONSTS:
    CCOL[_n] = _at
    _at += _w
NCONST = _at


def constants():
    c = np.zeros((P, NCONST), np.float32)

    def put(name, a):
        c[:, CCOL[name]:CCOL[name] + a.shape[1]] = a
    put("ident", np.eye(P))
    put("ones1024", np.full((P, P), 1 / 1024))
    put("ones512", np.full((P, P), 1 / 512))
    put("ones128", np.full((P, P), 1 / 128))
    put("ones64", np.kron(np.eye(2), np.full((64, 64), 1 / 64)))
    i, j = np.arange(T)[:, None], np.arange(T)[None, :]
    dist = np.where(j // 64 <= i // 64, np.abs(i - j), MASKED)
    causal = np.where(j <= i, 0, -MASKED)
    put("dist", np.concatenate([dist[:P, :P], dist[P:]], 1))
    put("distT", np.concatenate([dist.T[:P], dist.T[P:, P:]], 1))
    put("causal", np.concatenate([causal[:P, :P], causal[P:]], 1))
    put("causalT", np.concatenate([causal.T[:P], causal.T[P:, P:]], 1))
    put("eps", np.tile(np.array([[EPS, 64 * EPS, EPS / (1 - LAMBDA_INIT) ** 2, 1.0, 0, 0, 0, 0]]), (P, 1)))
    return c


class Phase:

    def __init__(self, name, n, blocks, ring0, out0):
        self.name, self.n, self.blocks, self.ring0, self.out0 = name, n, blocks, ring0, out0
        self.per = len(blocks)
        self.outs = n // self.per
        self.body = 12 if self.per == 3 else min(RING, n)
        self.turns = n // self.body

    def tile(self, i, c):
        g = self.ring0 + c
        return g % RING, g // RING + (self.body // RING) * i, g + self.body * i

    def out(self, i, c):
        return self.out0 + c // self.per + (self.body // self.per) * i


def phases():
    at, out, all_ = 0, 0, {}
    for name, n, blocks in PHASES:
        p = all_[name] = Phase(name, n, blocks, at, out)
        at, out = at + n, out + p.outs
    return all_, at


def program(nc, x_in, mem_in, params_in, consts_in, w, out):
    f32, f32r = mybir.dt.float32, mybir.dt.float32r
    ALU, ACT = mybir.AluOpType, mybir.ActivationFunctionType
    AX = mybir.AxisListType.X
    PH, NRING = phases()
    MUL, ADD, SUB = ALU.mult, ALU.add, ALU.subtract
    ds = bass.ds

    with ExitStack() as ctx:
        def sb(name, cols, dt=f32, rows=P):
            return ctx.enter_context(nc.sbuf_tensor(name, [rows, cols], dt))

        def sem(name):
            return ctx.enter_context(nc.semaphore(name))

        ring_raw = sb("ring_raw", RING * DM)
        ring_hi = sb("ring_hi", RING * DM, f32r)
        ring_lo = sb("ring_lo", RING * DM, f32r)
        act_hi = sb("act_hi", FT * T, f32r)
        act_lo = sb("act_lo", FT * T, f32r)
        xw_hi = sb("xw_hi", KT * T, f32r)
        xw_lo = sb("xw_lo", KT * T, f32r)
        x = sb("x", KT * T)
        u = sb("u", 44 * T)
        v_tok = sb("v_tok", 2 * DM)
        x_tok = sb("x_tok", 2 * DM)
        par = sb("par", NPARAM)
        con = sb("con", NCONST)
        t1, t2, t3 = sb("t1", 1024), sb("t2", 1024), sb("t3", 1024)
        scratch = sb("scratch", 4 * T)
        sq = scratch[:, 0:2 * T]
        sqsum = scratch[:, 2 * T:3 * T]
        sd = scratch[:, 3 * T:4 * T]
        small = scratch[0:64, :]
        rstd = sb("rstd", T)
        cb = u[:, 16 * T:19 * T]
        small_tok = sb("small_tok", 256)
        halo = sb("halo", 2 * 264)
        negmax, rowsum, rrow = sb("negmax", 4), sb("rowsum", 4), sb("rrow", 4)
        lam = sb("lam", 8)
        bank = [ctx.enter_context(nc.psum_tensor(f"bank{b}", [P, 512], f32)) for b in range(8)]

        gate, gate_s = t1, t2
        val, prod = t3, t1

        w_loaded = [sem(f"w_loaded{s}") for s in range(RING)]
        hi_done = sem("hi_done")
        lo_done = sem("lo_done")
        tile_done = sem("tile_done")
        out_ready = sem("out_ready")
        inputs = sem("inputs")
        x_loaded, mem_loaded = sem("x_loaded"), sem("mem_loaded")
        sq_done, ss_done = sem("sq_done"), sem("ss_done")
        xh_done, xl_done = sem("xh_done"), sem("xl_done")
        ms_done, sd_done, rstd_done = sem("ms_done"), sem("sd_done"), sem("rstd_done")
        halo_zero = sem("halo_zero")
        conv_a, conv_b = sem("conv_a"), sem("conv_b")
        conv_c, conv_d, conv_silu = sem("conv_c"), sem("conv_d"), sem("conv_silu")
        silu_done, val_done, prod_done = sem("silu_done"), sem("val_done"), sem("prod_done")
        ffn_hi, ffn_lo = sem("ffn_hi"), sem("ffn_lo")
        np_sq, np_ms, np_sd, np_rc, np_out = (sem(f"norm_{s}") for s in ("sq", "ms", "sd", "rc", "out"))
        tr_ps, tr_out = sem("tr_ps"), sem("tr_out")
        r_dec, r_s, r_pt, r_o, r_out = (sem(f"ret_{s}") for s in ("dec", "s", "pt", "o", "out"))
        r_gate, r_gated = sem("ret_gate"), sem("ret_gated")
        sm_s, sm_b, sm_m, sm_e = (sem(f"soft_{s}") for s in ("s", "b", "m", "e"))
        sm_r, sm_n, sm_t, sm_pt, sm_o, sm_out = (sem(f"soft_{s}") for s in ("r", "n", "t", "pt", "o", "out"))
        mix_hi, mix_lo = sem("mix_hi"), sem("mix_lo")
        lam_in, lam_ps, lam_e, lam_done = sem("lam_in"), sem("lam_ps"), sem("lam_e"), sem("lam_done")
        sm_zero = sem("small_zero")
        dve_small, act_small, pe_small = sem("dve_small"), sem("act_small"), sem("pe_small")
        cb_ps, cb_done = sem("cb_ps"), sem("cb_done")
        ss_bc, ss_b, ss_e, ss_p, ss_y, ss_s, ss_g = (sem(f"ssd_{s}") for s in ("bc", "b", "e", "p", "y", "s", "g"))
        gn_sq, gn_ms, gn_sd, gn_rc, gn_out = (sem(f"group_{s}") for s in ("sq", "ms", "sd", "rc", "out"))
        z_silu = sem("z_silu")
        stored = sem("stored")

        block = ctx.enter_context(nc.Block())

        def tile(buf, k, width=T):
            return buf[:, ds(k * T, width)]

        def pcol(name, k=0, rows=P):
            return par[0:rows, ds(k + PCOL[name], 1)]

        def cmat(name, width=P):
            return con[:, CCOL[name]:CCOL[name] + width]

        def eps(which, rows=P):
            return con[0:rows, CCOL["eps"] + which:CCOL["eps"] + which + 1]

        def half(buf, n, width=512):
            return buf[:, (n % 2) * 512:(n % 2) * 512 + width]

        def tok(buf, c0, width, tt):
            return buf[:, tt * DM + c0:tt * DM + c0 + width]

        NORMS = [("mem", act_hi, act_lo), ("attn0", xw_hi, xw_lo), ("ffn0", xw_hi, xw_lo), ("attn1", xw_hi, xw_lo),
                 ("ffn1", xw_hi, xw_lo), ("mix2", xw_hi, xw_lo), ("ffn2", xw_hi, xw_lo)]
        NORM_PHASE = ["kv", "in0", "up0", "in1", "up1", "in2", "up2"]
        c2 = 1 / (1 - LAMBDA_INIT) ** 2
        q64, o64, o128, l128 = ("ones64", 64.0, 1), ("ones64", 1.0, 0), ("ones128", 1.0, 0), ("ones128", c2, 2)
        PAIRS = {"L0": [(20, o64, "memk0", 0), (24, o64, "memk1", 0), (18, q64, "memq0", 0)],
                 "L0o": [(37 + 2 * n, o128, "gn", 2 * n) for n in range(3)],
                 "L1": [(2 * n, q64, "diffq", 0) for n in range(3)] + [(6 + 2 * n, o64, "diffk", 0) for n in range(3)]
                 + [(18, q64, "memq1", 0)],
                 "L1o": [(6 + 2 * n, l128, "subln", 0) for n in range(3)],
                 "L2": [(20 + 2 * n, q64, "foxq", 0) for n in range(4)] + [(28 + 2 * n, o64, "foxk", 0) for n in range(4)]}
        PAIR0, at = {}, 0
        for key, pairs in PAIRS.items():
            PAIR0[key] = at
            at += len(pairs)
        TURNS = {"L0": [(6 + n, v_tok, n * P) for n in range(6)] + [(22 + n, x_tok, n * P) for n in range(2)],
                 "L1": [(12 + n, v_tok, n * P) for n in range(6)] + [(26 + n, x_tok, n * P) for n in range(2)],
                 "L2": [(8 + n, x_tok, n * P) for n in range(8)] + [(36 + n, v_tok, n * P) for n in range(8)]}
        TURN0 = {"L0": 0, "L1": 8, "L2": 16}
        UNITS = {"L0": [("mem", h, 0) for h in range(4)],
                 "L1": [("diff", h, m) for h in range(6) for m in range(2)] + [("mem", h, 0) for h in range(4)],
                 "L2": [("fox", h, 0) for h in range(16)]}
        UNIT0 = {"L0": 0, "L1": 4, "L2": 20}
        HEAD0 = {"L0": 0, "L1": 4, "L2": 14}
        FILL0 = {"L0": 0, "L1": 2, "L2": 10}
        MIXED = {"L0": [18, 19] + [37 + n for n in range(6)], "L1": [18, 19] + [6 + n for n in range(6)],
                 "L2": [8 + n for n in range(8)] + [20 + n for n in range(8)]}
        SLOT = {"L0": [6, 7, 0, 1, 2, 3, 4, 5], "L1": [6, 7, 0, 1, 2, 3, 4, 5], "L2": list(range(16))}
        MIX0 = {"L0": 0, "L1": 8, "L2": 16}
        U_OUT0 = {"L0": PH["in0"].out0, "L1": PH["in1"].out0, "L2": PH["in2"].out0}
        KV_TILE = 20
        LG = [math.log(float(np.float32(1.0) - np.float32(2.0) ** np.float32(-5.0 - h))) for h in range(RET_HEADS)]
        DECAY = 28 * T
        SLOPE = [2.0 ** (-8.0 * (h + 1) / DIFF_HEADS) for h in range(DIFF_HEADS)]

        def units(L):
            out_, hd = [], HEAD0[L]
            for n, (kind, h, m) in enumerate(UNITS[L]):
                ends = kind != "diff" or m == 1
                out_.append((UNIT0[L] + n, kind, h, m, hd, ends))
                hd += ends
            return out_

        def fill_of(L, kind, h):
            if kind == "diff":
                return FILL0[L] + h, 6 + h, True
            if kind == "mem":
                return FILL0[L] + (6 if L == "L1" else 0) + h // 2, 18 + h // 2, h % 2 == 1
            return FILL0[L] + h // 2, 20 + h // 2, h % 2 == 1

        def fills_before(L, kind, h):
            return fill_of(L, kind, h)[0]

        @block.sync
        def _(sp):
            sp.dma_start(con[:, :], consts_in).then_inc(inputs, 16)
            sp.dma_start(par[:, :], params_in).then_inc(inputs, 16)
            sp.dma_start(u[:, 0:KT * T], mem_in).then_inc(mem_loaded, 16)

            def load(ph, i, c, first):
                slot, _, g = ph.tile(i, c)
                if not (first and ph.ring0 + c < RING):
                    sp.wait_ge(lo_done, g - RING + 1)
                width = ph.blocks[c % ph.per] * P
                row = (c // ph.per + (ph.body // ph.per) * i) * P
                col = (c % ph.per) * DM
                sp.dma_start(ring_raw[:, slot * DM:slot * DM + width],
                             w[ph.name][ds(row, P), col:col + width]).then_inc(w_loaded[slot], 16)

            for name, _, _ in PHASES:
                ph = PH[name]
                for c in range(ph.body):
                    load(ph, 0, c, True)
                if name == "kv":
                    sp.dma_start(x[:, :], x_in).then_inc(x_loaded, 16)
                if ph.turns > 1:
                    with sp.Fori(1, ph.turns) as i:
                        for c in range(ph.body):
                            load(ph, i, c, False)
            last = PH["down2"]
            for m in range(KT):
                sp.wait_ge(out_ready, last.out0 + m + 1)
                sp.dma_start(out[:, m * T:(m + 1) * T], tile(x, m)).then_inc(stored, 16)
            sp.wait_ge(stored, 16 * KT)

        @block.tensor
        def _(pe):
            mm = nc.tensor.matmul

            def project(ph, i, c, first, hi, lo, ready):
                slot, _, g = ph.tile(i, c)
                n = ph.out(i, c)
                b = (ph.out0 + c // ph.per) % 2
                part = c % ph.per
                pe.wait_ge(lo_done, g + 1)
                if part == 0 and not (first and n < 2):
                    pe.wait_ge(out_ready, n - 1)
                last = None
                for k in range(ph.blocks[part]):
                    kk = part * 8 + k
                    if first and c < ph.per:
                        ready(kk)
                    a = slot * DM + k * P
                    w_hi, w_lo = ring_hi[:, a:a + P], ring_lo[:, a:a + P]
                    end = part == ph.per - 1 and k == ph.blocks[part] - 1
                    mm(bank[b][:, 0:T], w_hi, tile(hi, kk), start=kk == 0, stop=False)
                    mm(bank[b][:, 0:T], w_hi, tile(lo, kk), start=False, stop=False)
                    last = mm(bank[b][:, 0:T], w_lo, tile(hi, kk), start=False, stop=end)
                last.then_inc(tile_done, 1)

            def mean_square(q):
                pe.wait_ge(ss_done, KT * (q + 1))
                mm(bank[7][:, 0:T], cmat("ones1024"), sqsum[:, :], start=True, stop=True).then_inc(ms_done, 1)

            def run(name, hi, lo, ready, q=None):
                ph = PH[name]
                for c in range(ph.body):
                    project(ph, 0, c, True, hi, lo, ready)
                    if c == 0 and q is not None:
                        mean_square(q)
                if ph.turns > 1:
                    with pe.Fori(1, ph.turns) as i:
                        for c in range(ph.body):
                            project(ph, i, c, False, hi, lo, ready)

            def stream_ready(q):
                return lambda k: pe.wait_ge(xl_done, KT * q + k + 1)

            def mixed_ready(L):
                return lambda k: pe.wait_ge(mix_lo, MIX0[L] + SLOT[L].index(k) + 1)

            def ffn_ready(layer):
                return lambda k: pe.wait_ge(ffn_lo, FT * layer + k + 1)

            def norm_pair(n, spec):
                pe.wait_ge(np_sq, n + 1)
                if n >= 2:
                    pe.wait_ge(np_sd, n - 1)
                mm(bank[2 + n % 2][:, :], cmat(spec[1][0]), half(t1, n), start=True, stop=True).then_inc(np_ms, 1)

            def turn(n, spec):
                if n >= 2:
                    pe.wait_ge(tr_out, n - 1)
                for tt in range(2):
                    last = nc.tensor.transpose(bank[4 + n % 2][:, tt * P:(tt + 1) * P],
                                               u[:, spec[0] * T + tt * P:spec[0] * T + (tt + 1) * P], cmat("ident"))
                last.then_inc(tr_ps, 1)

            def keys_first(bk, k_rows, q_rows, done):
                mm(bk[:, 0:T], k_rows[:, 0:P], q_rows[:, 0:T], start=True, stop=True)
                mm(bk[:, T:T + P], k_rows[:, P:T], q_rows[:, P:T], start=True, stop=True).then_inc(done, 1)

            def values_causal(o, v0, v1, probs, done):
                mm(o[:, 0:T], v0, probs[:, 0:T], start=True, stop=False)
                mm(o[:, P:T], v1, probs[:, T:T + P], start=False, stop=True).then_inc(done, 1)

            def ret_scores(h):
                if h >= 2:
                    pe.wait_ge(r_pt, h - 1)
                r0 = 64 * (h % 2)
                keys_first(bank[2 + h % 2], u[r0:r0 + 64, (3 + h // 2) * T:(4 + h // 2) * T],
                           u[r0:r0 + 64, (h // 2) * T:(h // 2 + 1) * T], r_s)

            def ret_values(h):
                pe.wait_ge(r_pt, h + 1)
                if h >= 2:
                    pe.wait_ge(r_out, h - 1)
                values_causal(bank[6 + h % 2], tok(v_tok, h * P, P, 0), tok(v_tok, h * P, P, 1), half(t1, h), r_o)

            def soft_scores(L, n, kind, h, m):
                if n >= 2:
                    pe.wait_ge(sm_e, n - 1)
                b = bank[2 + n % 2]
                if kind == "mem":
                    r0, q0, k0 = 64 * (h % 2), 18 + h // 2, KV_TILE + (0 if L == "L0" else 4) + h // 2
                    for it in range(2):
                        last = mm(b[:, it * T:(it + 1) * T], u[r0:r0 + 64, q0 * T + it * P:q0 * T + (it + 1) * P],
                                  u[r0:r0 + 64, k0 * T:(k0 + 1) * T], start=True, stop=True)
                    last.then_inc(sm_s, 1)
                    return
                if kind == "diff":
                    r0, q0, k0 = 64 * m, h, 6 + h
                else:
                    r0, q0, k0 = 64 * (h % 2), 20 + h // 2, 28 + h // 2
                fox = kind == "fox"
                for it, (a, width) in enumerate([(0, P), (P, T)]):
                    last = mm(b[:, a:a + width], u[r0:r0 + 64, q0 * T + it * P:q0 * T + (it + 1) * P],
                              u[r0:r0 + 64, k0 * T:k0 * T + width], start=True, stop=not fox)
                    if fox:
                        pick = con[32:48, CCOL["ident"] + 32 + h:CCOL["ident"] + 33 + h].to_broadcast([16, P])
                        last = mm(b[:, a:a + width], pick, small[32:48, T:T + width], start=False, stop=True)
                last.then_inc(sm_s, 1)

            def soft_turn(n, kind, hd):
                pe.wait_ge(sm_n, hd + 1)
                if hd >= 2:
                    pe.wait_ge(sm_pt, hd - 1)
                b, p = bank[4 + hd % 2], half(t2, n)
                if kind == "mem":
                    for it in range(2):
                        for jt in range(2):
                            last = nc.tensor.transpose(b[:, jt * T + it * P:jt * T + (it + 1) * P],
                                                       p[:, it * T + jt * P:it * T + (jt + 1) * P], cmat("ident"))
                else:
                    for s in range(3):
                        last = nc.tensor.transpose(b[:, s * P:(s + 1) * P], p[:, s * P:(s + 1) * P], cmat("ident"))
                last.then_inc(sm_t, 1)

            def soft_values(L, kind, h, hd):
                f, _, _ = fill_of(L, kind, h)
                pe.wait_ge(sm_pt, hd + 1)
                if f >= 2:
                    pe.wait_ge(sm_out, f - 1)
                o, p = bank[6 + f % 2], half(t3, hd)
                if kind == "diff":
                    values_causal(o, tok(v_tok, h * P, P, 0), tok(v_tok, h * P, P, 1), p, sm_o)
                    return
                o = o[64 * (h % 2):64 * (h % 2) + 64, :]
                if kind == "fox":
                    values_causal(o, tok(v_tok, h * 64, 64, 0), tok(v_tok, h * 64, 64, 1), p, sm_o)
                    return
                mm(o[:, 0:T], tok(x_tok, h * 64, 64, 0), p[:, 0:T], start=True, stop=False)
                mm(o[:, 0:T], tok(x_tok, h * 64, 64, 1), p[:, T:2 * T], start=False, stop=True).then_inc(sm_o, 1)

            def attend(L):
                todo = units(L)
                soft_scores(L, *todo[0][:4])
                behind = None
                for n, (g, kind, h, m, hd, ends) in enumerate(todo):
                    if n + 1 < len(todo):
                        soft_scores(L, *todo[n + 1][:4])
                    if ends:
                        soft_turn(g, kind, hd)
                        if behind:
                            soft_values(L, *behind)
                        behind = (kind, h, hd)
                soft_values(L, *behind)

            pe.wait_ge(inputs, 32)
            run("kv", act_hi, act_lo, stream_ready(0), 0)

            run("in0", xw_hi, xw_lo, stream_ready(1), 1)
            pe.wait_ge(out_ready, PH["in0"].out0 + 20)
            for n, spec in enumerate(PAIRS["L0"]):
                norm_pair(PAIR0["L0"] + n, spec)
            for n, spec in enumerate(TURNS["L0"]):
                turn(TURN0["L0"] + n, spec)
            pe.wait_ge(np_sd, 3)
            pe.wait_ge(tr_out, 8)
            pe.wait_ge(sd_done, 2)
            ret_scores(0)
            for h in range(RET_HEADS):
                if h + 1 < RET_HEADS:
                    ret_scores(h + 1)
                ret_values(h)
            pe.wait_ge(np_out, 3)
            pe.wait_ge(r_pt, 6)
            pe.wait_ge(r_out, 6)
            attend("L0")
            for n, spec in enumerate(PAIRS["L0o"]):
                if n == 0:
                    pe.wait_ge(sm_e, 4)
                norm_pair(PAIR0["L0o"] + n, spec)
            run("out0", act_hi, act_lo, mixed_ready("L0"))
            run("up0", xw_hi, xw_lo, stream_ready(2), 2)
            run("down0", act_hi, act_lo, ffn_ready(0))

            run("in1", xw_hi, xw_lo, stream_ready(3), 3)
            pe.wait_ge(out_ready, PH["in1"].out0 + 20)
            pe.wait_ge(lam_in, 1)
            mm(bank[6][:, 0:2], con[0:64, CCOL["ones1024"]:CCOL["ones1024"] + P], lam[0:64, 0:2],
               start=True, stop=True).then_inc(lam_ps, 1)
            for n, spec in enumerate(PAIRS["L1"]):
                norm_pair(PAIR0["L1"] + n, spec)
            for n, spec in enumerate(TURNS["L1"]):
                turn(TURN0["L1"] + n, spec)
            pe.wait_ge(np_out, PAIR0["L1o"])
            pe.wait_ge(tr_out, 16)
            pe.wait_ge(sd_done, 4)
            pe.wait_ge(lam_e, 1)
            attend("L1")
            for n, spec in enumerate(PAIRS["L1o"]):
                if n == 0:
                    pe.wait_ge(sm_e, UNIT0["L2"])
                norm_pair(PAIR0["L1o"] + n, spec)
            run("out1", act_hi, act_lo, mixed_ready("L1"))
            run("up1", xw_hi, xw_lo, stream_ready(4), 4)
            run("down1", act_hi, act_lo, ffn_ready(1))

            run("in2", xw_hi, xw_lo, stream_ready(5), 5)
            run("dtf", xw_hi, xw_lo, stream_ready(5))
            pe.wait_ge(out_ready, PH["dtf"].out0)
            for n, spec in enumerate(PAIRS["L2"]):
                norm_pair(PAIR0["L2"] + n, spec)
            pe.wait_ge(conv_silu, 12)
            for n, spec in enumerate(TURNS["L2"]):
                turn(TURN0["L2"] + n, spec)
            pe.wait_ge(tr_out, 32)
            for g in range(2):
                keys_first(bank[4 + g], u[:, (16 + g) * T:(17 + g) * T], u[:, (18 + g) * T:(19 + g) * T], cb_ps)
            pe.wait_ge(sd_done, 6)
            pe.wait_ge(dve_small, 9)
            for tt in range(2):
                nc.tensor.transpose(bank[6][:, tt * 64:(tt + 1) * 64], small[:, tt * P:(tt + 1) * P],
                                    con[0:64, CCOL["ident"]:CCOL["ident"] + 64])
            for tt in range(2):
                last = nc.tensor.transpose(bank[6][:, P + tt * 64:P + (tt + 1) * 64],
                                           small[:, 2 * T + tt * P:2 * T + (tt + 1) * P],
                                           con[0:64, CCOL["ident"]:CCOL["ident"] + 64])
            last.then_inc(pe_small, 1)

            def ssd_decay(h):
                if h >= 2:
                    pe.wait_ge(ss_b, h - 1)
                pick = con[0:16, CCOL["ident"] + h:CCOL["ident"] + h + 1].to_broadcast([16, P])
                mm(bank[2 + h % 2][:, 0:T], pick, small[0:16, 0:T], start=True, stop=True).then_inc(ss_bc, 1)

            def ssd_values(h):
                pe.wait_ge(ss_p, h + 1)
                if h // 2 >= 2:
                    pe.wait_ge(ss_s, h // 2 - 1)
                o = bank[6 + (h // 2) % 2][64 * (h % 2):64 * (h % 2) + 64, :]
                values_causal(o, tok(x_tok, h * 64, 64, 0), tok(x_tok, h * 64, 64, 1), half(t2, h), ss_y)

            pe.wait_ge(np_sd, PAIR0["L2"] + 8)
            pe.wait_ge(act_small, 4)
            ssd_decay(0)
            for h in range(SSD_HEADS):
                if h + 1 < SSD_HEADS:
                    ssd_decay(h + 1)
                ssd_values(h)
            pe.wait_ge(cb_done, 2)
            for t in range(8):
                pe.wait_ge(gn_sq, t + 1)
                mm(bank[4 + t // 4][:, 0:T], cmat("ones512"), t3[:, (t % 4) * T:(t % 4 + 1) * T],
                   start=t % 4 == 0, stop=t % 4 == 3).then_inc(gn_ms, 1)
            pe.wait_ge(np_out, PAIR0["L2"] + 8)
            pe.wait_ge(ss_b, 16)
            pe.wait_ge(gn_sd, 2)
            pe.wait_ge(ss_s, 8)
            attend("L2")
            run("out2", act_hi, act_lo, mixed_ready("L2"))
            run("up2", xw_hi, xw_lo, stream_ready(6), 6)
            run("down2", act_hi, act_lo, ffn_ready(2))

        @block.scalar
        def _(act):
            A = nc.scalar.activation

            def split_hi(ph, i, c, first=False):
                g0 = ph.ring0 + c + AHEAD
                slot, use, g = g0 % RING, g0 // RING + (ph.body // RING) * i, g0 + ph.body * i
                if first and g >= NRING:
                    return
                act.wait_ge(w_loaded[slot], 16 * (use + 1))
                if not (first and g < RING):
                    act.wait_ge(tile_done, g - RING + 1)
                A(ring_hi[:, slot * DM:(slot + 1) * DM], ring_raw[:, slot * DM:(slot + 1) * DM],
                  ACT.Copy).then_inc(hi_done, 1)

            def stream(q, m, src, ready):
                r = KT * q + m
                name, hi, _ = NORMS[q]
                ready()
                if r >= 2:
                    act.wait_ge(ss_done, r - 1)
                A(sq[:, (r % 2) * T:(r % 2 + 1) * T], tile(src, m), ACT.Square).then_inc(sq_done, 1)
                A(tile(hi, m), tile(src, m), ACT.Copy, scale=pcol(name, m)).then_inc(xh_done, 1)

            def root(q):
                act.wait_ge(ms_done, q + 1)
                A(sd[:, :], bank[7][:, 0:T], ACT.Sqrt, bias=eps(0)).then_inc(sd_done, 1)

            def run(name, after=None, q=None, unrolled=False):
                ph = PH[name]
                peeled = ph.turns if unrolled else 1
                for i in range(peeled):
                    for c in range(ph.body):
                        split_hi(ph, i, c, True)
                        if c == 0 and i == 0 and q is not None:
                            root(q)
                        if after:
                            after(ph, i, c)
                if peeled < ph.turns:
                    with act.Fori(peeled, ph.turns) as i:
                        for c in range(ph.body):
                            split_hi(ph, i, c)
                            if after:
                                after(ph, i, c)

            def into_stream(q):
                def after(ph, i, c):
                    if c % ph.per == ph.per - 1:
                        m = ph.out(i, c) - ph.out0
                        n = ph.out(i, c)
                        stream(q, m, x, lambda: act.wait_ge(out_ready, n + 1))
                return after

            def swiglu(layer):
                def after(ph, i, c):
                    p = FT * layer + 2 * i + c // 2
                    h = c // 2
                    n = ph.out(i, c)
                    if c % 2 == 0:
                        act.wait_ge(out_ready, n + 1)
                        if not (type(p) is int and p < 2):
                            act.wait_ge(prod_done, p - 1)
                        A(gate_s[:, h * T:(h + 1) * T], gate[:, h * T:(h + 1) * T], ACT.Silu).then_inc(silu_done, 1)
                    else:
                        ffn_split(p, h, 2 * i + c // 2)
                return after

            def ffn_split(p, h, f):
                act.wait_ge(prod_done, p + 1)
                A(tile(act_hi, f), prod[:, 512 + h * T:512 + (h + 1) * T], ACT.Copy).then_inc(ffn_hi, 1)

            def conv_first(n, taps, j, n_conv, par2):
                act.wait_ge(out_ready, n + 1)
                if not (type(n_conv) is int and n_conv < 2):
                    act.wait_ge(conv_b, n_conv - 1)
                wname, bname = ("conv4", "convb") if taps == 4 else ("conv3", "conv3b")
                A(t3[:, par2 * T:(par2 + 1) * T], halo[:, par2 * 264 + 4:par2 * 264 + 260], ACT.Identity,
                  scale=pcol(wname, j * taps + taps - 1), bias=pcol(bname, j)).then_inc(conv_a, 1)

            def conv_swiglu(ph, i, c):
                j = 4 * i + c
                n_conv = 12 + j
                conv_first(ph.out(i, c), 3, j, n_conv, c % 2)
                p = 2 * FT + 2 * i + c // 2
                h = c // 2
                if c % 2 == 0:
                    act.wait_ge(conv_d, n_conv + 1)
                    act.wait_ge(prod_done, p - 1)
                    A(gate_s[:, h * T:(h + 1) * T], t1[:, 0:T], ACT.Silu).then_inc(silu_done, 1)
                else:
                    ffn_split(p, h, 2 * i + c // 2)

            def ssd_in(ph, i, c):
                t = 4 * i + c
                if t < 8:
                    act.wait_ge(out_ready, ph.out0 + t + 1)
                    A(tile(u, t), tile(u, t), ACT.Silu).then_inc(z_silu, 1)
                elif t < 20:
                    j = t - 8
                    conv_first(ph.out(i, c), 4, j, j, j % 2)
                    act.wait_ge(conv_d, j + 1)
                    A(tile(u, t), t1[:, (j % 2) * T:(j % 2 + 1) * T], ACT.Silu).then_inc(conv_silu, 1)

            def norm_pair_sq(n, spec):
                if n >= 2:
                    act.wait_ge(np_ms, n - 1)
                A(half(t1, n), u[:, spec[0] * T:(spec[0] + 2) * T], ACT.Square).then_inc(np_sq, 1)

            def norm_pair_sd(n, spec):
                act.wait_ge(np_ms, n + 1)
                if n >= 2:
                    act.wait_ge(np_out, n - 1)
                _, scale, e = spec[1]
                A(half(t2, n), bank[2 + n % 2][:, :], ACT.Sqrt, scale=scale, bias=eps(e)).then_inc(np_sd, 1)

            def norm_pairs(key):
                specs = PAIRS[key]
                n0 = PAIR0[key]
                norm_pair_sq(n0, specs[0])
                for n, spec in enumerate(specs):
                    if n + 1 < len(specs):
                        norm_pair_sq(n0 + n + 1, specs[n + 1])
                    norm_pair_sd(n0 + n, spec)

            def turns(L):
                for n, (_, dst, c0) in enumerate(TURNS[L]):
                    g = TURN0[L] + n
                    act.wait_ge(tr_ps, g + 1)
                    A(dst[:, :].rearrange("p (t c) -> p t c", t=2)[:, :, c0:c0 + P],
                      bank[4 + g % 2][:, 0:T].rearrange("p (t c) -> p t c", t=2), ACT.Copy).then_inc(tr_out, 1)

            def soft_exp(n, kind):
                act.wait_ge(sm_m, n + 1)
                src = bank[2 + n % 2] if kind == "mem" else half(t1, n)
                p = half(t2, n)
                for it, (a, width) in enumerate([(0, T), (T, T)] if kind == "mem" else [(0, P), (P, T)]):
                    c = 2 * (n % 2) + it
                    last = A(p[:, a:a + width], src[:, a:a + width], ACT.Exp, bias=negmax[:, c:c + 1],
                             accum_out=rowsum[:, c:c + 1])
                last.then_inc(sm_e, 1)

            def soft_evac(kind, hd):
                act.wait_ge(sm_t, hd + 1)
                if hd >= 2:
                    act.wait_ge(sm_o, hd - 1)
                width = 512 if kind == "mem" else 384
                A(half(t3, hd, width), bank[4 + hd % 2][:, 0:width], ACT.Copy).then_inc(sm_pt, 1)

            def attend(L):
                todo = units(L)

                def exp(n):
                    if n >= 2:
                        _, kind, _, m, hd, _ = todo[n - 2]
                        if kind == "diff" and m == 0:
                            act.wait_ge(sm_n, hd + 1)
                        else:
                            act.wait_ge(sm_t, hd + 1)
                    soft_exp(*todo[n][:2])
                exp(0)
                for n, (g, kind, h, m, hd, ends) in enumerate(todo):
                    if n + 1 < len(todo):
                        exp(n + 1)
                    if ends:
                        soft_evac(kind, hd)

            def mix_split(L, order):
                for o in order:
                    A(tile(act_hi, SLOT[L][o]), tile(u, MIXED[L][o]), ACT.Copy).then_inc(mix_hi, 1)

            act.wait_ge(inputs, 32)
            act.wait_ge(mem_loaded, 16)
            for m in range(KT):
                stream(0, m, u, lambda: None)
            first = PH["kv"]
            for g in range(AHEAD):
                split_hi(first, 0, g - AHEAD, True)

            def kv_after(ph, i, c):
                if i == 0:
                    for m in (2 * c, 2 * c + 1):
                        stream(1, m, x, lambda: act.wait_ge(x_loaded, 16))
            run("kv", kv_after, 0, unrolled=True)

            run("in0", None, 1)
            for h in range(RET_HEADS):
                A(u[:, DECAY + h * 384:DECAY + (h + 1) * 384], cmat("distT", 384), ACT.Exp, scale=LG[h]).then_inc(r_dec, 1)
            act.wait_ge(out_ready, PH["in0"].out0 + 20)
            A(u[:, 12 * T:18 * T], u[:, 12 * T:18 * T], ACT.Silu).then_inc(r_gate, 1)
            norm_pairs("L0")
            turns("L0")
            for h in range(RET_HEADS):
                act.wait_ge(r_o, h + 1)
                A(tile(u, 37 + h), bank[6 + h % 2][:, 0:T], ACT.Copy).then_inc(r_out, 1)
            act.wait_ge(np_out, 3)
            attend("L0")
            act.wait_ge(r_o, 6)
            act.wait_ge(sm_t, 4)
            act.wait_ge(r_out, 6)
            norm_pairs("L0o")
            act.wait_ge(sm_out, 2)
            mix_split("L0", [0, 1])
            act.wait_ge(r_gated, 3)
            mix_split("L0", range(2, 8))
            run("out0", into_stream(2), unrolled=True)
            run("up0", swiglu(0), 2)
            run("down0", into_stream(3), unrolled=True)

            run("in1", None, 3)
            act.wait_ge(lam_ps, 1)
            A(lam[:, 2:4], bank[6][:, 0:2], ACT.Exp, scale=1024.0).then_inc(lam_e, 1)
            act.wait_ge(out_ready, PH["in1"].out0 + 20)
            norm_pairs("L1")
            turns("L1")
            act.wait_ge(np_out, PAIR0["L1o"])
            attend("L1")
            act.wait_ge(sm_t, HEAD0["L2"])
            act.wait_ge(sm_out, FILL0["L2"])
            norm_pairs("L1o")
            mix_split("L1", [0, 1])
            act.wait_ge(np_out, PAIR0["L2"])
            mix_split("L1", range(2, 8))
            run("out1", into_stream(4), unrolled=True)
            run("up1", swiglu(1), 4)
            run("down1", into_stream(5), unrolled=True)

            run("in2", ssd_in, 5, unrolled=True)
            run("dtf")
            norm_pairs("L2")
            turns("L2")
            act.wait_ge(cb_ps, 2)
            for g in range(2):
                A(cb[:, g * 384:(g + 1) * 384], bank[4 + g][:, 0:384], ACT.Copy).then_inc(cb_done, 1)
            act.wait_ge(dve_small, 3)
            A(small[:, T:2 * T], small[:, T:2 * T], ACT.Exp).then_inc(act_small, 1)
            act.wait_ge(act_small, 1)
            A(small[:, T:2 * T], small[:, T:2 * T], ACT.Ln, bias=eps(3, 64)).then_inc(act_small, 1)
            A(lam[0:64, 5:6], pcol("a_log", 0, 64), ACT.Exp).then_inc(act_small, 1)
            act.wait_ge(pe_small, 1)
            A(small_tok[:, :], bank[6][:, 0:256], ACT.Copy).then_inc(act_small, 1)
            for h in range(SSD_HEADS):
                act.wait_ge(ss_b, h + 1)
                A(half(t1, h, 384), half(t1, h, 384), ACT.Exp).then_inc(ss_e, 1)
            for t in range(8):
                act.wait_ge(ss_g, t + 1)
                if t >= 4:
                    act.wait_ge(gn_ms, t - 3)
                A(t3[:, (t % 4) * T:(t % 4 + 1) * T], tile(u, 8 + t), ACT.Square).then_inc(gn_sq, 1)
            act.wait_ge(ss_y, 16)
            for g in range(2):
                act.wait_ge(gn_ms, 4 * g + 4)
                A(t2[:, g * T:(g + 1) * T], bank[4 + g][:, 0:T], ACT.Sqrt, bias=eps(0)).then_inc(gn_sd, 1)
            act.wait_ge(gn_out, 8)
            mix_split("L2", range(8))
            attend("L2")
            act.wait_ge(sm_out, FILL0["L2"] + 8)
            mix_split("L2", range(8, 16))
            run("out2", into_stream(6), unrolled=True)
            run("up2", conv_swiglu, 6)
            run("down2", None, unrolled=True)

        @block.gpsimd
        def _(pool):
            def squares(q, m):
                r = KT * q + m
                pool.wait_ge(sq_done, r + 1)
                s = sq[:, (r % 2) * T:(r % 2 + 1) * T]
                if m == 0:
                    if q:
                        pool.wait_ge(ms_done, q)
                    nc.gpsimd.tensor_copy(sqsum[:, :], s).then_inc(ss_done, 1)
                else:
                    pool.wait_ge(ss_done, r)
                    nc.gpsimd.tensor_tensor(sqsum[:, :], sqsum[:, :], s, ADD).then_inc(ss_done, 1)

            def ffn(layer):
                def lo(i, h):
                    f = 2 * i + h
                    pool.wait_ge(ffn_hi, FT * layer + f + 1)
                    nc.gpsimd.tensor_tensor(tile(act_lo, f), prod[:, 512 + h * T:512 + (h + 1) * T],
                                            tile(act_hi, f).bitcast(f32), SUB).then_inc(ffn_lo, 1)
                with pool.Fori(0, FT // 2) as i:
                    for h in range(2):
                        lo(i, h)

            def mix_lo_parts(L):
                for o, t in enumerate(MIXED[L]):
                    pool.wait_ge(mix_hi, MIX0[L] + o + 1)
                    nc.gpsimd.tensor_tensor(tile(act_lo, SLOT[L][o]), tile(u, t),
                                            tile(act_hi, SLOT[L][o]).bitcast(f32), SUB).then_inc(mix_lo, 1)

            for q in (0, 1):
                for m in range(KT):
                    squares(q, m)
            for layer in range(3):
                mix_lo_parts(f"L{layer}")
                for m in range(KT):
                    squares(2 + 2 * layer, m)
                ffn(layer)
                if layer < 2:
                    for m in range(KT):
                        squares(3 + 2 * layer, m)

        @block.vector
        def _(dve):
            V = nc.vector

            def split_lo(ph, i, c, first=False):
                g0 = ph.ring0 + c + AHEAD
                slot, g = g0 % RING, g0 + ph.body * i
                if first and g >= NRING:
                    return
                dve.wait_ge(hi_done, g + 1)
                a, b = slot * DM, (slot + 1) * DM
                V.tensor_tensor(ring_lo[:, a:b], ring_raw[:, a:b], ring_hi[:, a:b].bitcast(f32), SUB).then_inc(lo_done, 1)

            def stream_lo(q, m, src):
                name, hi, lo = NORMS[q]
                dve.wait_ge(xh_done, KT * q + m + 1)
                V.scalar_tensor_tensor(tile(lo, m), tile(src, m), pcol(name, m), tile(hi, m).bitcast(f32),
                                       MUL, SUB).then_inc(xl_done, 1)

            def invert(q):
                dve.wait_ge(sd_done, q + 1)
                if q:
                    dve.wait_ge(out_ready, PH[NORM_PHASE[q]].out0)
                V.reciprocal(rstd[:, :], sd[:, :]).then_inc(rstd_done, 1)
                dve.wait_ge(rstd_done, q + 1)

            def run(name, evac, after=None, q=None, unrolled=False):
                ph = PH[name]
                peeled = ph.turns if unrolled else 1

                def step(i, c, first):
                    if c % ph.per == ph.per - 1:
                        if first and i == 0 and c == 0 and q is not None:
                            invert(q)
                        g = ph.tile(i, c)[2]
                        dve.wait_ge(tile_done, g + 1)
                        evac(ph, i, c, bank[(ph.out0 + c // ph.per) % 2][:, 0:T])
                    split_lo(ph, i, c, first)
                    if after:
                        after(ph, i, c)
                for i in range(peeled):
                    for c in range(ph.body):
                        step(i, c, True)
                if peeled < ph.turns:
                    with dve.Fori(peeled, ph.turns) as i:
                        for c in range(ph.body):
                            step(i, c, False)

            def scaled_into(dst0):
                def evac(ph, i, c, ps):
                    V.tensor_tensor(tile(u, ph.out(i, c) - ph.out0 + dst0), ps, rstd[:, :], MUL).then_inc(out_ready, 1)
                return evac

            def add_to_x(ph, i, c, ps):
                m = ph.out(i, c) - ph.out0
                V.tensor_tensor(tile(x, m), tile(x, m), ps, ADD).then_inc(out_ready, 1)

            def into_stream(q):
                def after(ph, i, c):
                    if c % ph.per == ph.per - 1:
                        stream_lo(q, ph.out(i, c) - ph.out0, x)
                return after

            def swiglu_evac(layer):
                def evac(ph, i, c, ps):
                    h = c // 2
                    p = FT * layer + 2 * i + h
                    if c % 2 == 0:
                        V.tensor_tensor(gate[:, h * T:(h + 1) * T], ps, rstd[:, :], MUL).then_inc(out_ready, 1)
                    else:
                        if not (layer == 0 and type(i) is int):
                            dve.wait_ge(prod_done, p - 1)
                        V.tensor_tensor(val[:, h * T:(h + 1) * T], ps, rstd[:, :], MUL).then_inc(out_ready, 1)
                return evac

            def product(p, h, v):
                dve.wait_ge(silu_done, p + 1)
                if not (type(p) is int and p < 2):
                    dve.wait_ge(ffn_lo, p - 1)
                V.tensor_tensor(prod[:, 512 + h * T:512 + (h + 1) * T], v, gate_s[:, h * T:(h + 1) * T],
                                MUL).then_inc(prod_done, 1)

            def swiglu_after(layer):
                def after(ph, i, c):
                    if c % 2 == 1:
                        h = c // 2
                        dve.wait_ge(out_ready, ph.out(i, c) + 1)
                        product(FT * layer + 2 * i + h, h, val[:, h * T:(h + 1) * T])
                return after

            def halo_evac(conv0, skip=None):
                def evac(ph, i, c, ps):
                    b = c % 2
                    V.tensor_tensor(halo[:, b * 264 + 4:b * 264 + 260], ps, rstd[:, :], MUL).then_inc(out_ready, 1)
                return evac

            def conv_rest(wname, taps, j, n_conv, b, into):
                dve.wait_ge(conv_a, n_conv + 1)
                chain = {4: [conv_b, conv_c, conv_d], 3: [conv_b, conv_d]}[taps]
                acc = t3[:, b * T:(b + 1) * T]
                bufs = [t3[:, (2 + b) * T:(3 + b) * T]] + ([t2[:, 512 + b * T:512 + (b + 1) * T]] if taps == 4 else []) + [into]
                for s, (done, dst) in enumerate(zip(chain, bufs)):
                    shift = s + 1
                    V.scalar_tensor_tensor(dst, halo[:, b * 264 + 4 - shift:b * 264 + 260 - shift],
                                           pcol(wname, j * taps + taps - 1 - shift), acc, MUL, ADD).then_inc(done, 1)
                    dve.wait_ge(done, n_conv + 1)
                    acc = dst

            def conv_swiglu(ph, i, c):
                j = 4 * i + c
                conv_rest("conv3", 3, j, 12 + j, c % 2, t1[:, (c % 2) * T:(c % 2 + 1) * T])
                if c % 2 == 1:
                    product(2 * FT + 2 * i + c // 2, c // 2, t1[:, T:2 * T])

            def in2_evac(ph, i, c, ps):
                t = 4 * i + c
                if 8 <= t < 20:
                    halo_evac(0)(ph, i, c, ps)
                else:
                    scaled_into(0)(ph, i, c, ps)

            def ssd_conv(ph, i, c):
                t = 4 * i + c
                if 8 <= t < 20:
                    j = t - 8
                    if j >= 2:
                        dve.wait_ge(conv_silu, j - 1)
                    conv_rest("conv4", 4, j, j, j % 2, t1[:, (j % 2) * T:(j % 2 + 1) * T])

            def norm_pair(n, spec):
                dve.wait_ge(np_sd, n + 1)
                V.reciprocal(half(t2, n), half(t2, n)).then_inc(np_rc, 1)
                dve.wait_ge(np_rc, n + 1)
                a, name, k = spec[0], spec[2], spec[3]
                if name == "gn":
                    for s in range(2):
                        last = V.scalar_tensor_tensor(tile(u, a + s), tile(u, a + s), pcol(name, k + s),
                                                      half(t2, n)[:, s * T:(s + 1) * T], MUL, MUL)
                else:
                    last = V.scalar_tensor_tensor(u[:, a * T:(a + 2) * T], u[:, a * T:(a + 2) * T], pcol(name, k),
                                                  half(t2, n), MUL, MUL)
                last.then_inc(np_out, 1)

            def soft_max(n, kind, h):
                dve.wait_ge(sm_s, n + 1)
                b, c = bank[2 + n % 2], 2 * (n % 2)
                if kind == "mem":
                    V.tensor_reduce(negmax[:, c:c + 2], b[:, :].rearrange("p (t c) -> p t c", t=2), AX, ALU.max,
                                    negate=True).then_inc(sm_m, 1)
                    return
                s = half(t1, n, 384)
                if kind == "diff":
                    V.scalar_tensor_tensor(s, cmat("dist", 384), -SLOPE[h], b[:, 0:384], MUL, ADD).then_inc(sm_b, 2)
                else:
                    for it, (a, width) in enumerate([(0, P), (P, T)]):
                        mask = con[:, CCOL["causal"] + a:CCOL["causal"] + a + width]
                        k = it * 64 + 32 + h
                        V.scalar_tensor_tensor(s[:, a:a + width], b[:, a:a + width], small_tok[:, k:k + 1], mask,
                                               ADD, ADD).then_inc(sm_b, 1)
                dve.wait_ge(sm_b, 2 * (n - (UNIT0["L1"] if n < UNIT0["L2"] else UNIT0["L2"] - 12)) + 2)
                for it, (a, width) in enumerate([(0, P), (P, T)]):
                    last = V.tensor_reduce(negmax[:, c + it:c + it + 1], s[:, a:a + width], AX, ALU.max, negate=True)
                last.then_inc(sm_m, 1)

            def soft_norm(n, kind, h, m, hd):
                dve.wait_ge(sm_e, n + 1)
                c = 2 * (n % 2)
                V.reciprocal(rrow[:, c:c + 2], rowsum[:, c:c + 2]).then_inc(sm_r, 1)
                p = half(t2, n)
                if kind == "diff":
                    if m == 0:
                        return
                    dve.wait_ge(sm_r, soft_count[0] + 1)
                    soft_count[0] += 1
                    V.tensor_scalar(rrow[:, c:c + 2], rrow[:, c:c + 2], lam[:, 4:5], None, MUL).then_inc(sm_r, 1)
                    dve.wait_ge(sm_r, soft_count[0] + 1)
                    soft_count[0] += 1
                    first, c0 = half(t2, n - 1), 2 * ((n - 1) % 2)
                    for it, (a, width) in enumerate([(0, P), (P, T)]):
                        V.tensor_scalar(p[:, a:a + width], p[:, a:a + width], rrow[:, c + it:c + it + 1], None,
                                        MUL).then_inc(sm_r, 1)
                    dve.wait_ge(sm_r, soft_count[0] + 2)
                    soft_count[0] += 2
                    for it, (a, width) in enumerate([(0, P), (P, T)]):
                        last = V.scalar_tensor_tensor(p[:, a:a + width], first[:, a:a + width], rrow[:, c0 + it:c0 + it + 1],
                                                      p[:, a:a + width], MUL, ADD)
                    last.then_inc(sm_n, 1)
                    return
                dve.wait_ge(sm_r, soft_count[0] + 1)
                soft_count[0] += 1
                for it, (a, width) in enumerate([(0, T), (T, T)] if kind == "mem" else [(0, P), (P, T)]):
                    last = V.tensor_scalar(p[:, a:a + width], p[:, a:a + width], rrow[:, c + it:c + it + 1], None, MUL)
                last.then_inc(sm_n, 1)

            soft_count = [0]

            def soft_out(L, kind, h, hd):
                f, t, full = fill_of(L, kind, h)
                if not full:
                    return
                dve.wait_ge(sm_o, hd + 1)
                V.tensor_copy(tile(u, t), bank[6 + f % 2][:, 0:T]).then_inc(sm_out, 1)

            def attend(L):
                todo = units(L)
                soft_max(*todo[0][:3])
                behind = None
                for n, (g, kind, h, m, hd, ends) in enumerate(todo):
                    if n + 1 < len(todo):
                        soft_max(*todo[n + 1][:3])
                    soft_norm(g, kind, h, m, hd)
                    if kind == "diff" and m == 0:
                        soft_count[0] += 1
                    if ends:
                        if behind:
                            soft_out(L, *behind)
                        behind = (kind, h, hd)
                soft_out(L, *behind)

            V.memset(halo[:, :], 0.0).then_inc(halo_zero, 1)
            dve.wait_ge(inputs, 32)
            for m in range(KT):
                stream_lo(0, m, u)
            for g in range(AHEAD):
                split_lo(PH["kv"], 0, g - AHEAD, True)

            def kv_after(ph, i, c):
                if i == 0:
                    for m in (2 * c, 2 * c + 1):
                        stream_lo(1, m, x)
            run("kv", scaled_into(KV_TILE), kv_after, 0, unrolled=True)

            run("in0", scaled_into(0), None, 1)
            for n, spec in enumerate(PAIRS["L0"]):
                norm_pair(PAIR0["L0"] + n, spec)
            for h in range(RET_HEADS):
                dve.wait_ge(r_s, h + 1)
                dve.wait_ge(r_dec, h + 1)
                if h >= 2:
                    dve.wait_ge(r_o, h - 1)
                V.scalar_tensor_tensor(half(t1, h, 384), bank[2 + h % 2][:, 0:384], 64.0 ** -0.5,
                                       u[:, DECAY + h * 384:DECAY + (h + 1) * 384], MUL, MUL).then_inc(r_pt, 1)
            attend("L0")
            dve.wait_ge(r_gate, 1)
            for n, spec in enumerate(PAIRS["L0o"]):
                norm_pair(PAIR0["L0o"] + n, spec)
                dve.wait_ge(np_out, PAIR0["L0o"] + n + 1)
                a, g = 37 + 2 * n, 12 + 2 * n
                V.tensor_tensor(u[:, a * T:(a + 2) * T], u[:, a * T:(a + 2) * T], u[:, g * T:(g + 2) * T],
                                MUL).then_inc(r_gated, 1)
            run("out0", add_to_x, into_stream(2), unrolled=True)
            run("up0", swiglu_evac(0), swiglu_after(0), 2)
            run("down0", add_to_x, into_stream(3), unrolled=True)

            lc = PCOL["lam"]
            for s in range(2):
                last = V.tensor_tensor(lam[0:64, s:s + 1], par[0:64, lc + 2 * s:lc + 2 * s + 1],
                                       par[0:64, lc + 2 * s + 1:lc + 2 * s + 2], MUL)
            last.then_inc(lam_in, 1)
            run("in1", scaled_into(0), None, 3)
            dve.wait_ge(lam_e, 1)
            V.tensor_scalar(lam[:, 4:5], lam[:, 3:4], lam[:, 2:3], LAMBDA_INIT, SUB, SUB).then_inc(lam_done, 1)
            dve.wait_ge(lam_done, 1)
            for n, spec in enumerate(PAIRS["L1"]):
                norm_pair(PAIR0["L1"] + n, spec)
            attend("L1")
            for n, spec in enumerate(PAIRS["L1o"]):
                norm_pair(PAIR0["L1o"] + n, spec)
            run("out1", add_to_x, into_stream(4), unrolled=True)
            run("up1", swiglu_evac(1), swiglu_after(1), 4)
            run("down1", add_to_x, into_stream(5), unrolled=True)

            dve.wait_ge(halo_zero, 1)
            run("in2", in2_evac, ssd_conv, 5, unrolled=True)

            def small_evac(ph, i, c, ps):
                V.tensor_tensor(small[:, 0:T], ps[0:64, :], rstd[0:64, :], MUL).then_inc(out_ready, 1)
            dve.wait_ge(ss_done, 6 * KT)
            dve.wait_ge(ms_done, 6)
            V.memset(small[:, :], 0.0).then_inc(sm_zero, 1)
            dve.wait_ge(sm_zero, 1)
            run("dtf", small_evac)
            dve.wait_ge(out_ready, PH["dtf"].out0 + 1)
            z, neg = small[:, 0:T], small[:, T:2 * T]
            V.tensor_scalar(z, z, pcol("small_b", 0, 64), None, ADD).then_inc(dve_small, 1)
            dve.wait_ge(dve_small, 1)
            V.scalar_tensor_tensor(neg, z, -1.0, z, MUL, ALU.min).then_inc(dve_small, 2)
            for n, spec in enumerate(PAIRS["L2"]):
                norm_pair(PAIR0["L2"] + n, spec)
            dve.wait_ge(act_small, 3)
            V.scalar_tensor_tensor(small[0:16, 2 * T:3 * T], z[0:16], 0.0, neg[0:16], ALU.max, ADD).then_inc(dve_small, 1)
            V.scalar_tensor_tensor(small[32:64, 3 * T:4 * T], z[32:64], 0.0, neg[32:64], ALU.min, SUB).then_inc(dve_small, 1)
            dve.wait_ge(dve_small, 5)
            V.tensor_scalar(small[0:16, 3 * T:4 * T], small[0:16, 2 * T:3 * T], lam[0:16, 5:6], -1.0, MUL, MUL).then_inc(dve_small, 1)
            V.memset(small[:, T:2 * T], 1.0).then_inc(dve_small, 1)
            dve.wait_ge(dve_small, 7)
            V.tensor_tensor_scan(small[:, 0:T], small[:, T:2 * T], small[:, 3 * T:4 * T], 0.0, MUL, ADD).then_inc(dve_small, 1)
            dve.wait_ge(dve_small, 8)
            V.tensor_scalar(small[:, T:2 * T], small[:, 0:T], -1.0, None, MUL).then_inc(dve_small, 1)
            dve.wait_ge(act_small, 4)
            dve.wait_ge(cb_done, 2)
            dve.wait_ge(z_silu, 8)

            def ssd_mask(h):
                dve.wait_ge(ss_bc, h + 1)
                if h >= 2:
                    dve.wait_ge(ss_p, h - 1)
                for st, (a, q0, width) in enumerate([(0, 0, T), (T, P, P)]):
                    k = st * 64 + h
                    last = V.scalar_tensor_tensor(t1[:, (h % 2) * 512 + a:(h % 2) * 512 + a + width],
                                                  bank[2 + h % 2][:, q0:q0 + width], small_tok[:, k:k + 1],
                                                  con[:, CCOL["causalT"] + a:CCOL["causalT"] + a + width], SUB, ADD)
                last.then_inc(ss_b, 1)

            def ssd_weights(h):
                dve.wait_ge(ss_e, h + 1)
                if h >= 2:
                    dve.wait_ge(ss_y, h - 1)
                g = h // 8
                for st, (a, width) in enumerate([(0, T), (T, P)]):
                    k = P + st * 64 + h
                    last = V.scalar_tensor_tensor(half(t2, h)[:, a:a + width], half(t1, h)[:, a:a + width],
                                                  small_tok[:, k:k + 1], cb[:, g * 384 + a:g * 384 + a + width], MUL, MUL)
                last.then_inc(ss_p, 1)

            def ssd_gate(t):
                dve.wait_ge(ss_y, 2 * t + 2)
                y = tile(u, 8 + t)
                V.scalar_tensor_tensor(y, y, pcol("skip", t), bank[6 + t % 2][:, 0:T], MUL, ADD).then_inc(ss_s, 1)
                dve.wait_ge(ss_s, t + 1)
                V.tensor_tensor(y, y, tile(u, t), MUL).then_inc(ss_g, 1)

            ssd_mask(0)
            for h in range(SSD_HEADS):
                if h + 1 < SSD_HEADS:
                    ssd_mask(h + 1)
                ssd_weights(h)
                if h % 2 == 0 and h >= 2:
                    ssd_gate(h // 2 - 1)
            ssd_gate(7)
            for g in range(2):
                dve.wait_ge(gn_sd, g + 1)
                r = t2[:, g * T:(g + 1) * T]
                V.reciprocal(r, r).then_inc(gn_rc, 1)
                dve.wait_ge(gn_rc, g + 1)
                for t in range(4 * g, 4 * g + 4):
                    y = tile(u, 8 + t)
                    V.scalar_tensor_tensor(y, y, pcol("ssdn", t), r, MUL, MUL).then_inc(gn_out, 1)
            attend("L2")
            run("out2", add_to_x, into_stream(6), unrolled=True)
            run("up2", halo_evac(12), conv_swiglu, 6)
            run("down2", add_to_x, None, unrolled=True)


def column_tiles(a):
    k, n = a.shape
    return np.ascontiguousarray(a.reshape(k // P, P, n // P, P).transpose(2, 1, 0, 3).reshape(n, k))


def features(a):
    return a.reshape(-1, P).T


def kernel(**inputs):
    import concourse.bacc as bacc
    from concourse.bass_utils import run_bass_kernel_spmd

    a = {k: np.ascontiguousarray(v) for k, v in inputs.items()}
    w = {}
    w["kv"] = np.concatenate([column_tiles(a["w_mem_kv"][l]) for l in range(2)])

    def interleaved(m, n):
        return column_tiles(m).reshape(2, n, P, -1).transpose(1, 0, 2, 3).reshape(2 * n * P, -1)
    for l in range(2):
        w[f"in{l}"] = column_tiles(a["w_in"][l])
        w[f"out{l}"] = column_tiles(a["w_out"][l])
        w[f"up{l}"] = interleaved(a["w_gate_up"][l], FT)
        w[f"down{l}"] = column_tiles(a["w_down"][l])
    w_in2 = a["w_in_2"][0]
    w["in2"] = column_tiles(np.concatenate([w_in2[:, 0:2560], w_in2[:, 2576:5648]], 1))
    small = np.zeros((DM, P), np.float32)
    small[:, 0:16] = w_in2[:, 2560:2576]
    small[:, 32:48] = w_in2[:, 5648:5664]
    w["dtf"] = column_tiles(small)
    w["out2"] = column_tiles(a["w_out_2"][0])
    w["up2"] = interleaved(a["w_up_2"][0], FT)
    w["down2"] = column_tiles(a["w_down_2"][0])

    par = np.zeros((P, NPARAM), np.float32)

    def put(name, v):
        par[0:v.shape[0], PCOL[name]:PCOL[name] + v.shape[1]] = v

    def twice(v):
        return np.concatenate([v, v]).reshape(P, 1)
    for l in range(2):
        put(f"attn{l}", features(a["attn_norm_w"][l]))
        put(f"ffn{l}", features(a["ffn_norm_w"][l]))
        put(f"memq{l}", twice(a["mem_q_norm_w"][l]))
        put(f"memk{l}", twice(a["mem_k_norm_w"][l]))
    put("mem", features(a["mem_norm_w"]))
    put("mix2", features(a["norm_mix_w_2"][0]))
    put("ffn2", features(a["norm_ffn_w_2"][0]))
    put("gn", features(a["ret_gn_w"][0]))
    put("diffq", twice(a["diff_q_norm_w"][0]))
    put("diffk", twice(a["diff_k_norm_w"][0]))
    put("subln", features(a["diff_subln_w"][0]))
    put("lam", np.stack([a[f"diff_lambda_{n}"][0] for n in ("q1", "k1", "q2", "k2")], 1))
    put("conv4", a["ssd_conv_w_2"][0].reshape(4, 12, P).transpose(2, 1, 0).reshape(P, 48))
    put("convb", features(a["ssd_conv_b_2"][0]))
    bias = np.zeros((64, 1), np.float32)
    bias[0:16, 0] = a["ssd_dt_bias_2"][0]
    bias[32:48, 0] = a["fox_f_bias_2"][0]
    put("small_b", bias)
    put("a_log", a["ssd_a_log_2"][0].reshape(16, 1))
    put("skip", features(np.repeat(a["ssd_d_2"][0], 64)))
    put("ssdn", features(a["ssd_norm_w_2"][0]))
    put("foxq", twice(a["fox_q_norm_w_2"][0]))
    put("foxk", twice(a["fox_k_norm_w_2"][0]))
    put("conv3", a["ffn_conv_w_2"][0].reshape(3, 2, FT, P).transpose(3, 2, 1, 0).reshape(P, 132))
    put("conv3b", a["ffn_conv_b_2"][0].reshape(2, FT, P).transpose(2, 1, 0).reshape(P, 44))

    def feature_major(m):
        return np.ascontiguousarray(m.reshape(T, KT, P).transpose(2, 1, 0).reshape(P, KT * T))

    arrays = {"x_in": feature_major(a["x"]), "mem_in": feature_major(a["mem"]), "params_in": par,
              "consts_in": constants()}
    arrays.update({f"w_{n}": np.ascontiguousarray(m) for n, m in w.items()})
    nc = bacc.Bacc("TRN2", target_bir_lowering=False, num_devices=1)
    ap = {n: nc.dram_tensor(n, list(m.shape), mybir.dt.float32, kind="ExternalInput").ap() for n, m in arrays.items()}
    out = nc.dram_tensor("out", [P, KT * T], mybir.dt.float32, kind="ExternalOutput").ap()
    program(nc, ap["x_in"], ap["mem_in"], ap["params_in"], ap["consts_in"], {n: ap[f"w_{n}"] for n in w}, out)
    r = run_bass_kernel_spmd(nc, [arrays], core_ids=[0])
    y = r.results[0]["out"]
    return y.reshape(P, KT, T).transpose(2, 1, 0).reshape(1, T, DM)
```

```python
import math
from contextlib import ExitStack

import numpy as np

import concourse.bass as bass
from concourse import mybir

P = 128
T = 256
DM = 1024
KT = DM // P
FF = 2816
FT = FF // P
RING = 4
AHEAD = 3
EPS = 1e-6
MASKED = 1e30
LAMBDA_INIT = 0.8 - 0.6 * math.exp(-0.3)
RET_HEADS = DIFF_HEADS = 6
SSD_HEADS = 16

PHASES = [("kv", 8, [8], 4),
          ("in0", 20, [8], 20), ("oa0", 8, [6], 8), ("ob0", 8, [2], 4), ("up0", 44, [8], 4), ("down0", 24, [8, 8, 6], 12),
          ("in1", 20, [8], 20), ("oa1", 8, [6], 8), ("ob1", 8, [2], 4), ("up1", 44, [8], 4), ("down1", 24, [8, 8, 6], 12),
          ("in2", 45, [8], 45), ("oa2", 16, [8, 6], 16), ("ob2", 8, [2], 4), ("up2", 44, [8], 4), ("down2", 24, [8, 8, 6], 12)]

OUT_INPUTS = {"oa0": [6, 7, 0, 1, 2, 3], "ob0": [4, 5], "oa1": [6, 7, 0, 1, 2, 3], "ob1": [4, 5],
              "oa2": list(range(14)), "ob2": [14, 15]}

SMALL = 44
ORDER = {"in0": [18, 19, 0, 3, 6, 7, 1, 4, 8, 9, 2, 5, 10, 11, 12, 13, 14, 15, 16, 17],
         "in1": [18, 19] + [t for j in range(3) for t in (2 * j, 2 * j + 1, 6 + 2 * j, 7 + 2 * j, 12 + 2 * j, 13 + 2 * j)],
         "in2": list(range(8, 20)) + [SMALL] + list(range(8))
         + [t for j in range(4) for t in (20 + 2 * j, 21 + 2 * j, 28 + 2 * j, 29 + 2 * j, 36 + 2 * j, 37 + 2 * j)]}

PARAMS = [("attn0", 8), ("attn1", 8), ("mem", 8), ("ffn0", 8), ("ffn1", 8), ("mix2", 8), ("ffn2", 8),
          ("memq0", 1), ("memq1", 1), ("memk0", 1), ("memk1", 1), ("gn", 6), ("diffq", 1), ("diffk", 1),
          ("subln", 1), ("lam", 4), ("conv4", 48), ("convb", 12), ("small_b", 1), ("a_log", 1),
          ("skip", 8), ("ssdn", 8), ("foxq", 1), ("foxk", 1), ("conv3", 132), ("conv3b", 44), ("eps", 4)]
PCOL, _at = {}, 0
for _n, _w in PARAMS:
    PCOL[_n] = _at
    _at += _w
NPARAM = _at

CONSTS = [("ident", 128), ("ones1024", 128), ("ones512", 128), ("ones128", 128), ("ones64", 128),
          ("dist", 384), ("distT", 384), ("causal", 384), ("causalT", 384)]
CCOL, _at = {}, 0
for _n, _w in CONSTS:
    CCOL[_n] = _at
    _at += _w
NCONST = _at


def constants():
    c = np.zeros((P, NCONST), np.float32)

    def put(name, a):
        c[:, CCOL[name]:CCOL[name] + a.shape[1]] = a
    put("ident", np.eye(P))
    put("ones1024", np.full((P, P), 1 / 1024))
    put("ones512", np.full((P, P), 1 / 512))
    put("ones128", np.full((P, P), 1 / 128))
    put("ones64", np.kron(np.eye(2), np.full((64, 64), 1 / 64)))
    i, j = np.arange(T)[:, None], np.arange(T)[None, :]
    dist = np.where(j // 64 <= i // 64, np.abs(i - j), MASKED)
    causal = np.where(j <= i, 0, -MASKED)
    put("dist", np.concatenate([dist[:P, :P], dist[P:]], 1))
    put("distT", np.concatenate([dist.T[:P], dist.T[P:, P:]], 1))
    put("causal", np.concatenate([causal[:P, :P], causal[P:]], 1))
    put("causalT", np.concatenate([causal.T[:P], causal.T[P:, P:]], 1))
    return c


class Phase:

    def __init__(self, name, n, blocks, body, ring0, out0):
        self.name, self.n, self.blocks, self.ring0, self.out0 = name, n, blocks, ring0, out0
        self.per = len(blocks)
        self.outs = n // self.per
        self.body, self.turns = body, n // body
        self.inputs = OUT_INPUTS.get(name, list(range(sum(blocks))))

    def tile(self, i, c):
        g = self.ring0 + c
        return g % RING, g + self.body * i

    def out(self, i, c):
        return self.out0 + c // self.per + (self.body // self.per) * i


def phases():
    at, out, all_, widths = 0, 0, {}, []
    for name, n, blocks, body in PHASES:
        p = all_[name] = Phase(name, n, blocks, body, at, out)
        at, out = at + n, out + p.outs
        widths += [b * P for b in blocks] * p.outs
    return all_, widths


def plans():
    plan = {0: [[] for _ in range(28)], 1: [[] for _ in range(28)], 2: [[] for _ in range(61)]}

    def at(layer, slot, kind, *key):
        plan[layer][slot].append((kind, *key))

    def norm(layer, slot, tile, soon=False):
        at(layer, slot, "squares", tile)
        at(layer, slot + 1, "norm", tile)
        if soon:
            plan[layer][slot + 2].insert(0, ("norm_soon", tile))
        else:
            plan[layer][slot + 3].insert(0, ("norm_out", tile))

    def unit(layer, slot, kind, h, maps=1):
        at(layer, slot + 2, "values", kind, h)
        for m in range(maps):
            at(layer, slot + 1, "softmax", kind, h, m)
        at(layer, slot + 1, "weights", kind, h)
        for m in range(maps):
            at(layer, slot, "scores", kind, h, m)

    for n, t in enumerate((22, 23, 26, 27)):
        at(0, n, "turn", t)
    for h in range(RET_HEADS):
        at(0, h, "decays", h)
    norm(0, 0, 20)
    norm(0, 2, 18)
    norm(0, 4, 24)
    for h in range(4):
        unit(0, 5 + h, "mem", h)
    for n, slot in enumerate((5, 6, 9, 10, 13, 14)):
        at(0, slot, "turn", 6 + n)
    for h, slot in enumerate((9, 10, 11, 12, 14, 15)):
        at(0, slot + 1, "ret_out", h)
        at(0, slot, "ret_scores", h)
    for k in (6, 7):
        at(0, 11, "mix", k)
    norm(0, 12, 37)
    norm(0, 14, 39)
    norm(0, 17, 41)
    for half_, slot in ((0, 19), (1, 19), (2, 20)):
        at(0, slot, "gate_silu", half_)
    for half_, slot in ((0, 19), (1, 19), (2, 20)):
        at(0, slot, "gated", half_)
        at(0, slot, "mix", 2 * half_)
        at(0, slot, "mix", 2 * half_ + 1)

    norm(1, 2, 18)
    norm(1, 4, 0)
    norm(1, 6, 6)
    for h in range(4):
        unit(1, 5 + h, "mem", h)
    for n, slot in enumerate((7, 8, 13, 14, 19, 20)):
        at(1, slot, "turn", 12 + n)
    for h, slot in enumerate((9, 10, 14, 15, 22, 23)):
        unit(1, slot, "diff", h, 2)
    for k in (6, 7):
        at(1, 11, "mix", k)
    norm(1, 9, 2)
    norm(1, 11, 8)
    norm(1, 13, 6 + 64)
    for k in (0, 1):
        at(1, 16, "mix", k)
    norm(1, 15, 4)
    norm(1, 17, 8 + 64, True)
    norm(1, 19, 10)
    for k in (2, 3):
        at(1, 19, "mix", k)
    norm(1, 25, 10 + 64, True)
    for k in (4, 5):
        at(1, 27, "mix", k)

    for t in range(8):
        at(2, 3 + t, "turn", 8 + t)
    at(2, 13, "cb", 0)
    for s in range(4):
        at(2, 13 + (s + 1) // 2, "small", s)
    for h in range(SSD_HEADS):
        at(2, 17 + h, "ssd_weights", h)
        at(2, 17 + h, "ssd_out", h)
        at(2, 16 + h, "ssd_scores", h)
    at(2, 21, "z_silu", 0)
    for t in range(8):
        at(2, max(22 + t, 19 + 2 * t), "ssd_gate", t)
        at(2, max(23 + t, 20 + 2 * t), "ssd_square", t)
    for j in range(4):
        a = 21 + 6 * j
        norm(2, a + 2, 20 + 2 * j)
        norm(2, a + 4, 28 + 2 * j)
        at(2, a + 5, "turn", 36 + 2 * j)
        at(2, a + 6, "turn", 37 + 2 * j)
        for h in range(4):
            unit(2, a + 7 + h, "fox", 4 * j + h)
        for n in range(2):
            at(2, a + 10 + 2 * n, "mix", 8 + 2 * j + n)
    for g, slot in ((0, 28), (1, 40)):
        at(2, slot, "group_norm", g)
        plan[2][slot + 1].insert(0, ("group_out", g))
        for k in range(4):
            at(2, slot + 2, "mix", 4 * g + k)
    return plan


def program(nc, x_in, mem_in, params_in, consts_in, w, out):
    f32, f32r = mybir.dt.float32, mybir.dt.float32r
    ALU, ACT = mybir.AluOpType, mybir.ActivationFunctionType
    AX = mybir.AxisListType.X
    PH, WIDTH = phases()
    PLAN = plans()
    NRING = len(WIDTH)
    MUL, ADD, SUB = ALU.mult, ALU.add, ALU.subtract
    ds = bass.ds

    with ExitStack() as ctx:
        def sb(name, cols, dt=f32):
            return ctx.enter_context(nc.sbuf_tensor(name, [P, cols], dt))

        def sem(name):
            return ctx.enter_context(nc.semaphore(name))

        ring_raw = sb("ring_raw", RING * DM)
        ring_hi = sb("ring_hi", RING * DM, f32r)
        ring_lo = sb("ring_lo", RING * DM, f32r)
        act_hi = sb("act_hi", FT * T, f32r)
        act_lo = sb("act_lo", FT * T, f32r)
        xw_hi = sb("xw_hi", KT * T, f32r)
        xw_lo = sb("xw_lo", KT * T, f32r)
        x = sb("x", KT * T)
        u = sb("u", 44 * T)
        v_tok = sb("v_tok", 2 * DM)
        x_tok = sb("x_tok", 2 * DM)
        par = sb("par", NPARAM)
        con = sb("con", NCONST)
        scratch = sb("scratch", 4 * T)
        sq = scratch[:, 0:2 * T]
        sqsum = scratch[:, 2 * T:3 * T]
        logs = scratch[:, 3 * T:4 * T]
        small = scratch[0:64, :]
        gsum, gsq = sqsum, logs
        cb = u[:, 16 * T:19 * T]
        rstd = sb("rstd", T)
        halo = sb("halo", 2 * 264)
        negmax, rowsum, rrow = sb("negmax", 4), sb("rowsum", 4), sb("rrow", 4)
        lam = sb("lam", 8)
        tmp = sb("tmp", 3072)
        roots_b = sb("roots_b", 512)
        bank = [ctx.enter_context(nc.psum_tensor(f"bank{b}", [P, 512], f32)) for b in range(8)]

        def normed(n):
            return roots_b[:, :] if n % 2 else tmp[:, 1024:1536]

        def probs(n, layer=0):
            return tmp[:, (n % 2) * 512:(n % 2) * 512 + (384 if layer == 2 else 512)]

        def probs_t(n, layer):
            a = (1536, 2688)[n % 2] if layer == 2 else 1536 + (n % 2) * 512
            return tmp[:, a:a + (384 if layer == 2 else 512)]

        def small_tok(k):
            a = 384 + k // P * 512 + k % P
            return tmp[:, a:a + 1]
        decayed = tmp[:, 2560:2944]

        def ssd_w(h):
            return tmp[:, 1920 + (h % 2) * 384:2304 + (h % 2) * 384]
        gate_s, gate, val, prod = (tmp[:, a:a + 512] for a in (0, 512, 1024, 1536))
        conv_out, tap_c, tap_a, tap_b = (tmp[:, a:a + 512] for a in (512, 1024, 2048, 2560))

        w_loaded = [sem(f"w_loaded{s}") for s in range(RING)]
        hi_done = sem("hi_done")
        lo_done = sem("lo_done")
        tile_done = sem("tile_done")
        out_ready = sem("out_ready")
        par_loaded, con_loaded = sem("par_loaded"), sem("con_loaded")
        x_loaded, mem_loaded = sem("x_loaded"), [sem("mem_loaded0"), sem("mem_loaded1")]
        sq_done, ss_done = sem("sq_done"), sem("ss_done")
        xh_done, xl_done = sem("xh_done"), sem("xl_done")
        ms_done, ln_done, root_done = sem("ms_done"), sem("ln_done"), sem("root_done")
        newton, rstd_done = sem("newton"), sem("rstd_done")
        halo_zero = sem("halo_zero")
        conv_a, conv_b = sem("conv_a"), sem("conv_b")
        conv_c, conv_d, conv_silu = sem("conv_c"), sem("conv_d"), sem("conv_silu")
        silu_done, prod_done = sem("silu_done"), sem("prod_done")
        ffn_hi, ffn_lo = sem("ffn_hi"), sem("ffn_lo")
        np_sq, np_ms, np_ln, np_rt, np_nt, np_out = (sem(f"norm_{s}") for s in ("sq", "ms", "ln", "rt", "nt", "out"))
        weighted = sem("weighted")
        tr_ps, tr_out = sem("tr_ps"), sem("tr_out")
        r_dec, r_s, r_pt, r_o, r_out = (sem(f"ret_{s}") for s in ("dec", "s", "pt", "o", "out"))
        r_gate, r_gated = sem("ret_gate"), sem("ret_gated")
        sm_s, sm_b, sm_m, sm_e = (sem(f"soft_{s}") for s in ("s", "b", "m", "e"))
        sm_r, sm_n, sm_t, sm_pt, sm_o, sm_out = (sem(f"soft_{s}") for s in ("r", "n", "t", "pt", "o", "out"))
        mix_hi, mix_lo = sem("mix_hi"), sem("mix_lo")
        lam_in, lam_ps, lam_e, lam_done = sem("lam_in"), sem("lam_ps"), sem("lam_e"), sem("lam_done")
        small_zero = sem("small_zero")
        dve_small, act_small, pe_small = sem("dve_small"), sem("act_small"), sem("pe_small")
        cb_ps, cb_done = sem("cb_ps"), sem("cb_done")
        ss_bc, ss_b, ss_e, ss_p, ss_y, ss_s, ss_g = (sem(f"ssd_{s}") for s in ("bc", "b", "e", "p", "y", "s", "g"))
        gs_sq, gs_sum = sem("group_sq"), sem("group_sum")
        z_silu = sem("z_silu")
        stored = sem("stored")

        block = ctx.enter_context(nc.Block())

        def tile(buf, k, width=T):
            return buf[:, ds(k * T, width)]

        def two(buf, h):
            return buf[:, h * T:(h + 1) * T]

        def pcol(name, k=0, rows=P):
            return par[0:rows, ds(k + PCOL[name], 1)]

        def cmat(name, width=P):
            return con[:, CCOL[name]:CCOL[name] + width]

        def eps(which, rows=P):
            return par[0:rows, PCOL["eps"] + which:PCOL["eps"] + which + 1]

        def tok(buf, c0, width, tt):
            return buf[:, tt * DM + c0:tt * DM + c0 + width]

        NORMS = [("mem", "kv", act_hi, act_lo), ("attn0", "in0", xw_hi, xw_lo), ("ffn0", "up0", xw_hi, xw_lo),
                 ("attn1", "in1", xw_hi, xw_lo), ("ffn1", "up1", xw_hi, xw_lo), ("mix2", "in2", xw_hi, xw_lo),
                 ("ffn2", "up2", xw_hi, xw_lo)]
        LAST_Q = {0: 1, 1: 3, 2: 5}
        OUT = 1 / (1 - LAMBDA_INIT) ** 2
        SPEC = {(0, 20): ("ones64", 1.0, 0, "memk0", 0), (0, 24): ("ones64", 1.0, 0, "memk1", 0),
                (0, 18): ("ones64", 64.0, 1, "memq0", 0), (1, 18): ("ones64", 64.0, 1, "memq1", 0)}
        for n in range(3):
            SPEC[0, 37 + 2 * n] = ("ones128", 1.0, 0, "gn", 2 * n)
            SPEC[1, 2 * n] = ("ones64", 64.0, 1, "diffq", 0)
            SPEC[1, 6 + 2 * n] = ("ones64", 1.0, 0, "diffk", 0)
            SPEC[1, 6 + 2 * n + 64] = ("ones128", OUT, 2, "subln", 0)
        for n in range(4):
            SPEC[2, 20 + 2 * n] = ("ones64", 64.0, 1, "foxq", 0)
            SPEC[2, 28 + 2 * n] = ("ones64", 1.0, 0, "foxk", 0)
        TURN = {(0, 22): (x_tok, 0), (0, 23): (x_tok, P), (0, 26): (x_tok, 2 * P), (0, 27): (x_tok, 3 * P)}
        for n in range(6):
            TURN[0, 6 + n] = TURN[1, 12 + n] = (v_tok, n * P)
        for n in range(8):
            TURN[2, 8 + n], TURN[2, 36 + n] = (x_tok, n * P), (v_tok, n * P)
        LG = [math.log(float(np.float32(1.0) - np.float32(2.0) ** np.float32(-5.0 - h))) for h in range(RET_HEADS)]
        DECAY = 28 * T
        SLOPE = [2.0 ** (-8.0 * (h + 1) / DIFF_HEADS) for h in range(DIFF_HEADS)]

        def filled(layer, kind, h):
            if kind == "diff":
                return 6 + h, True
            return (18 if kind == "mem" else 20) + h // 2, h % 2 == 1

        number, so_far = {}, {}

        def count(name, key):
            number[name, key] = so_far.get(name, 0)
            so_far[name] = so_far.get(name, 0) + 1
        for layer in range(3):
            for steps in PLAN[layer]:
                for kind, *key in steps:
                    k = (layer, *key)
                    count("norm" if kind == "group_norm" else kind, (kind, *k) if kind in ("norm", "group_norm") else k)
                    if kind == "values" and filled(layer, key[0], key[1])[1]:
                        count("fill", (layer, filled(layer, key[0], key[1])[0]))
                    if kind == "scores" and key[0] != "mem":
                        count("biased", k)

        def norm_no(layer, t):
            return number["norm", ("norm", layer, t)]

        def norm_of(layer, t):
            for a in (t, t - 1):
                if ("norm", ("norm", layer, a)) in number:
                    return norm_no(layer, a)
            return None

        def arrived(eng, layer, t):
            if t >= 64 or (layer == 0 and 37 <= t < 43):
                if layer == 0:
                    eng.wait_ge(r_out, t - 37 + 2)
                else:
                    eng.wait_ge(sm_out, number["fill", (1, t - 64 + 1)] + 1)
            elif layer == 0 and 20 <= t < 28:
                eng.wait_ge(out_ready, t + 1 - 20 + 0 if t % 2 else t + 2 - 20)
            elif layer == 2 and 8 <= t < 20:
                eng.wait_ge(conv_silu, t - 8 + 1)
            else:
                order = ORDER[f"in{layer}"]
                last = order.index(t)
                eng.wait_ge(out_ready, PH[f"in{layer}"].out0 + last + 1)

        def mixed_tile(eng, layer, k):
            if layer < 2:
                t = 12 + k if k >= 6 else (37 + k if layer == 0 else 6 + k)
            else:
                t = 8 + k if k < 8 else 12 + k
            if eng is None:
                return t
            if layer == 2 and k < 8:
                eng.wait_ge(np_out, number["norm", ("group_norm", 2, k // 4)] + 1)
            elif layer == 0 and k < 6:
                eng.wait_ge(r_gated, k // 2 + 1)
            elif layer == 1 and k < 6:
                eng.wait_ge(np_out, norm_no(1, 64 + 6 + k // 2 * 2) + 1)
            else:
                eng.wait_ge(sm_out, number["fill", (layer, t)] + 1)
            return t

        unit_head, unit_ends = {}, {}
        for (name_, key_), n_ in number.items():
            if name_ == "scores":
                unit_head[n_] = number["weights", key_[:3]]
                unit_ends[n_] = key_[1] != "diff" or key_[3] == 1

        @block.sync
        def _(sp):
            def load(ph, i, c, body):
                slot = (ph.ring0 + c) % RING
                g = ph.ring0 + c + body * i
                if not (type(i) is int and g < RING):
                    sp.wait_ge(lo_done, g - RING + 1)
                width = ph.blocks[c % ph.per] * P
                row = (c // ph.per + (body // ph.per) * i) * P
                col = (c % ph.per) * DM
                sp.dma_start(ring_raw[:, slot * DM:slot * DM + width],
                             w[ph.name][ds(row, P), col:col + width]).then_inc(w_loaded[slot], 16)

            sp.dma_start(par[:, :], params_in).then_inc(par_loaded, 16)
            half_w = KT * T // 2
            sp.dma_start(u[:, 0:half_w], mem_in[:, 0:half_w]).then_inc(mem_loaded[0], 16)
            load(PH["kv"], 0, 0, 4)
            sp.dma_start(u[:, half_w:2 * half_w], mem_in[:, half_w:2 * half_w]).then_inc(mem_loaded[1], 16)
            load(PH["kv"], 0, 1, 4)
            sp.dma_start(con[:, :], consts_in).then_inc(con_loaded, 16)
            load(PH["kv"], 0, 2, 4)
            sp.dma_start(x[:, :], x_in).then_inc(x_loaded, 16)
            load(PH["kv"], 0, 3, 4)
            for name, n, _, _ in PHASES:
                ph = PH[name]
                body = 12 if ph.per == 3 else 4
                start = 1 if name == "kv" else 0
                if n // body - start > 1:
                    with sp.Fori(start, n // body) as i:
                        for c in range(body):
                            load(ph, i, c, body)
                elif n // body > start:
                    for c in range(body):
                        load(ph, start, c, body)
                for c in range(n // body * body, n):
                    load(ph, 0, c, n)
            last = PH["down2"]
            for m in range(KT):
                sp.wait_ge(out_ready, last.out0 + m + 1)
                sp.dma_start(out[:, m * T:(m + 1) * T], tile(x, m)).then_inc(stored, 16)
            sp.wait_ge(stored, 16 * KT)

        @block.tensor
        def _(pe):
            mm = nc.tensor.matmul

            def project(ph, i, c, hi, lo, ready):
                slot, g = ph.tile(i, c)
                n = ph.out(i, c)
                b = (ph.out0 + c // ph.per) % 2
                part = c % ph.per
                first = type(i) is int and i == 0
                pe.wait_ge(lo_done, g + 1)
                if part == 0 and not (first and n < 2):
                    pe.wait_ge(out_ready, n - 1)
                last = None
                for k in range(ph.blocks[part]):
                    kk = part * 8 + k
                    t = ph.inputs[kk]
                    if first and c < ph.per:
                        ready(t)
                    a = slot * DM + k * P
                    w_hi, w_lo = ring_hi[:, a:a + P], ring_lo[:, a:a + P]
                    end = part == ph.per - 1 and k == ph.blocks[part] - 1
                    mm(bank[b][:, 0:T], w_hi, tile(hi, t), start=kk == 0, stop=False)
                    mm(bank[b][:, 0:T], w_hi, tile(lo, t), start=False, stop=False)
                    last = mm(bank[b][:, 0:T], w_lo, tile(hi, t), start=False, stop=end)
                last.then_inc(tile_done, 1)

            def mean_square(q):
                if q == 0:
                    pe.wait_ge(con_loaded, 16)
                pe.wait_ge(ss_done, KT * (q + 1))
                mm(bank[7][:, 0:T], cmat("ones1024"), sqsum, start=True, stop=True).then_inc(ms_done, 1)

            def run(name, hi, lo, ready, q=None, then=None):
                ph = PH[name]
                for c in range(ph.body):
                    project(ph, 0, c, hi, lo, ready)
                    if c == 0 and q is not None:
                        mean_square(q)
                    if then:
                        then(c)
                if ph.turns > 1:
                    with pe.Fori(1, ph.turns) as i:
                        for c in range(ph.body):
                            project(ph, i, c, hi, lo, ready)

            def stream_ready(q):
                return lambda k: pe.wait_ge(xl_done, KT * q + k + 1)

            def mixed_ready(layer):
                return lambda k: pe.wait_ge(mix_lo, number["mix", (layer, k)] + 1)

            def ffn_ready(layer):
                return lambda k: pe.wait_ge(ffn_lo, FT * layer + k + 1)

            issued = {"norm": 0, "turn": 0, "weights": 0}

            def bank4_free():
                if issued["norm"]:
                    pe.wait_ge(np_out, issued["norm"])

            def bank5_free():
                if issued["turn"]:
                    pe.wait_ge(tr_out, issued["turn"])
                if issued["weights"]:
                    pe.wait_ge(sm_pt, issued["weights"])

            def norm(layer, t):
                n = norm_no(layer, t)
                pe.wait_ge(np_sq, number["squares", (layer, t)] + 1)
                bank4_free()
                if (layer, t) == (2, 20):
                    pe.wait_ge(act_small, 4)
                mm(bank[4][:, :], cmat(SPEC[layer, t][0]), normed(n), start=True, stop=True).then_inc(np_ms, 1)
                issued["norm"] = n + 1

            def group_norm(layer, g):
                pe.wait_ge(gs_sum, 4 * g + 4)
                bank4_free()
                mm(bank[4][:, 0:T], cmat("ones512"), gsum, start=True, stop=True).then_inc(np_ms, 1)
                issued["norm"] += 1

            def turn(layer, t):
                arrived(pe, layer, t)
                bank5_free()
                for tt in range(2):
                    last = nc.tensor.transpose(bank[5][:, tt * P:(tt + 1) * P],
                                               u[:, t * T + tt * P:t * T + (tt + 1) * P], cmat("ident"))
                last.then_inc(tr_ps, 1)
                issued["turn"] += 1

            def keys_first(bk, k_rows, q_rows, done):
                mm(bk[:, 0:T], k_rows[:, 0:P], q_rows[:, 0:T], start=True, stop=True)
                mm(bk[:, T:T + P], k_rows[:, P:T], q_rows[:, P:T], start=True, stop=True).then_inc(done, 1)

            def values_causal(o, v0, v1, p, done):
                mm(o[:, 0:T], v0, p[:, 0:T], start=True, stop=False)
                mm(o[:, P:T], v1, p[:, T:T + P], start=False, stop=True).then_inc(done, 1)

            def ret_scores(layer, h):
                arrived(pe, 0, 3 + h // 2)
                if h == 0:
                    pe.wait_ge(rstd_done, 2)
                else:
                    pe.wait_ge(r_pt, h)
                r0 = 64 * (h % 2)
                keys_first(bank[7], u[r0:r0 + 64, (3 + h // 2) * T:(4 + h // 2) * T],
                           u[r0:r0 + 64, (h // 2) * T:(h // 2 + 1) * T], r_s)

            def ret_out(layer, h):
                pe.wait_ge(r_pt, h + 1)
                pe.wait_ge(tr_out, number["turn", (0, 6 + h)] + 1)
                pe.wait_ge(sm_out, 2)
                if h:
                    pe.wait_ge(r_out, h)
                values_causal(bank[6], tok(v_tok, h * P, P, 0), tok(v_tok, h * P, P, 1), decayed, r_o)

            def scores(layer, kind, h, m):
                n = number["scores", (layer, kind, h, m)]
                if kind == "mem":
                    q0, k0, r0 = 18 + h // 2, (20 if layer == 0 else 24) + h // 2, 64 * (h % 2)
                    pe.wait_ge(np_out, norm_of(0, k0) + 1)
                elif kind == "diff":
                    q0, k0, r0 = h, 6 + h, 64 * m
                    pe.wait_ge(np_out, norm_of(1, k0) + 1)
                else:
                    q0, k0, r0 = 20 + h // 2, 28 + h // 2, 64 * (h % 2)
                    pe.wait_ge(np_out, norm_of(2, k0) + 1)
                pe.wait_ge(np_out, norm_of(layer, q0) + 1)
                if layer == 2:
                    pe.wait_ge(sm_e, n)
                elif n >= 2:
                    pe.wait_ge(sm_e, n - 1)
                b = bank[2 if layer == 2 else 2 + n % 2]
                for it, (a, width) in enumerate([(0, T), (T, T)] if kind == "mem" else [(0, P), (P, T)]):
                    last = mm(b[:, a:a + width], u[r0:r0 + 64, q0 * T + it * P:q0 * T + (it + 1) * P],
                              u[r0:r0 + 64, k0 * T:k0 * T + width], start=True, stop=kind != "fox")
                    if kind == "fox":
                        pick = con[32:48, CCOL["ident"] + 32 + h:CCOL["ident"] + 33 + h].to_broadcast([16, P])
                        last = mm(b[:, a:a + width], pick, small[32:48, T:T + width], start=False, stop=True)
                last.then_inc(sm_s, 1)

            def weights(layer, kind, h):
                hd = number["weights", (layer, kind, h)]
                n = number["scores", (layer, kind, h, 1 if kind == "diff" else 0)]
                pe.wait_ge(sm_n, hd + 1)
                bank5_free()
                issued["weights"] = hd + 1
                if layer == 2 and h == 0:
                    pe.wait_ge(cb_done, 2)
                p = probs(n, layer)
                blocks_ = [0, 2, 1, 3] if kind == "mem" else [0, 1, 2]
                for s, d in enumerate(blocks_):
                    last = nc.tensor.transpose(bank[5][:, d * P:(d + 1) * P], p[:, s * P:(s + 1) * P], cmat("ident"))
                last.then_inc(sm_t, 1)

            def values(layer, kind, h):
                hd = number["weights", (layer, kind, h)]
                t, full = filled(layer, kind, h)
                f = number["fill", (layer, t)]
                pe.wait_ge(sm_pt, hd + 1)
                if f:
                    pe.wait_ge(sm_out, f)
                o, p = bank[6], probs_t(hd, layer)
                if kind == "diff":
                    pe.wait_ge(tr_out, number["turn", (1, 12 + h)] + 1)
                    values_causal(o, tok(v_tok, h * P, P, 0), tok(v_tok, h * P, P, 1), p, sm_o)
                    return
                o = o[64 * (h % 2):64 * (h % 2) + 64, :]
                if kind == "fox":
                    pe.wait_ge(tr_out, number["turn", (2, 36 + h // 2)] + 1)
                    values_causal(o, tok(v_tok, h * 64, 64, 0), tok(v_tok, h * 64, 64, 1), p, sm_o)
                    return
                c0 = (0 if layer == 0 else 2 * P) + h * 64
                pe.wait_ge(tr_out, number["turn", (0, (22 if layer == 0 else 26) + h // 2)] + 1)
                mm(o[:, 0:T], tok(x_tok, c0, 64, 0), p[:, 0:T], start=True, stop=False)
                mm(o[:, 0:T], tok(x_tok, c0, 64, 1), p[:, T:2 * T], start=False, stop=True).then_inc(sm_o, 1)

            def c_times_b(layer, _):
                bank4_free()
                bank5_free()
                for g in range(2):
                    arrived(pe, 2, 18 + g)
                    keys_first(bank[4 + g], u[:, (16 + g) * T:(17 + g) * T], u[:, (18 + g) * T:(19 + g) * T], cb_ps)

            def small_steps(layer, s):
                if s != 3:
                    return
                pe.wait_ge(cb_done, 2)
                pe.wait_ge(dve_small, 9)
                ident = con[0:64, CCOL["ident"]:CCOL["ident"] + 64]
                for k, c0 in enumerate((0, 2 * T)):
                    for tt in range(2):
                        last = nc.tensor.transpose(bank[4][:, k * P + tt * 64:k * P + (tt + 1) * 64],
                                                   small[:, c0 + tt * P:c0 + (tt + 1) * P], ident)
                last.then_inc(pe_small, 1)

            def ssd_scores(layer, h):
                if h:
                    pe.wait_ge(ss_b, h)
                pick = con[0:16, CCOL["ident"] + h:CCOL["ident"] + h + 1].to_broadcast([16, P])
                mm(bank[3][:, 0:T], pick, small[0:16, 0:T], start=True, stop=True).then_inc(ss_bc, 1)

            def ssd_out(layer, h):
                pe.wait_ge(ss_p, h + 1)
                if h % 2 == 0 and h:
                    pe.wait_ge(ss_s, h // 2)
                o = bank[7][64 * (h % 2):64 * (h % 2) + 64, :]
                values_causal(o, tok(x_tok, h * 64, 64, 0), tok(x_tok, h * 64, 64, 1), ssd_w(h), ss_y)

            DO = {"norm": norm, "group_norm": group_norm, "turn": turn, "ret_scores": ret_scores, "ret_out": ret_out,
                  "scores": scores, "weights": weights, "values": values, "cb": c_times_b, "small": small_steps,
                  "ssd_scores": ssd_scores, "ssd_out": ssd_out}

            def follow(layer, slot0):
                def then(c):
                    for kind, *key in PLAN[layer][slot0 + c]:
                        if kind in DO:
                            DO[kind](layer, *key)
                return then

            run("kv", act_hi, act_lo, stream_ready(0), 0)
            for layer in range(3):
                q = LAST_Q[layer]
                if layer == 1:
                    pe.wait_ge(lam_in, 1)
                    mm(bank[5][:, 0:2], con[0:64, CCOL["ones1024"]:CCOL["ones1024"] + P], lam[0:64, 0:2],
                       start=True, stop=True).then_inc(lam_ps, 1)
                    pe.wait_ge(lam_e, 1)
                n_in = PH[f"in{layer}"].n
                run(f"in{layer}", xw_hi, xw_lo, stream_ready(q), q, follow(layer, 0))
                run(f"oa{layer}", act_hi, act_lo, mixed_ready(layer), None, follow(layer, n_in))
                run(f"ob{layer}", act_hi, act_lo, mixed_ready(layer))
                run(f"up{layer}", xw_hi, xw_lo, stream_ready(q + 1), q + 1)
                run(f"down{layer}", act_hi, act_lo, ffn_ready(layer))

        @block.scalar
        def _(act):
            A = nc.scalar.activation

            def split_hi(ph, i, c):
                g0 = ph.ring0 + c + AHEAD
                slot, use, g = g0 % RING, g0 // RING + (ph.body // RING) * i, g0 + ph.body * i
                known = type(i) is int
                if known:
                    if g >= NRING:
                        return
                    use = g // RING
                    slot = g % RING
                width = WIDTH[g] if known else DM
                act.wait_ge(w_loaded[slot], 16 * (use + 1))
                if not (known and g < RING):
                    act.wait_ge(tile_done, g - RING + 1)
                A(ring_hi[:, slot * DM:slot * DM + width], ring_raw[:, slot * DM:slot * DM + width],
                  ACT.Copy).then_inc(hi_done, 1)

            def stream(q, m, src):
                r = KT * q + m
                name, _, hi, _ = NORMS[q]
                if r >= 2:
                    act.wait_ge(ss_done, r - 1)
                if q == 6 and m == 0:
                    act.wait_ge(mix_lo, so_far["mix"])
                A(two(sq, r % 2), tile(src, m), ACT.Square).then_inc(sq_done, 1)
                A(tile(hi, m), tile(src, m), ACT.Copy, scale=pcol(name, m)).then_inc(xh_done, 1)

            def inverse_root(q):
                act.wait_ge(ms_done, q + 1)
                A(logs, bank[7][:, 0:T], ACT.Ln, bias=eps(0)).then_inc(ln_done, 1)
                act.wait_ge(ln_done, q + 1)
                if q:
                    act.wait_ge(out_ready, PH[NORMS[q][1]].out0)
                A(rstd[:, :], logs, ACT.Exp, scale=-0.5).then_inc(root_done, 1)

            def run(name, after=None, q=None, unrolled=False, end=None):
                ph = PH[name]
                peeled = ph.turns if unrolled else 1
                for i in range(peeled):
                    for c in range(ph.body):
                        split_hi(ph, i, c)
                        if c == 0 and i == 0 and q is not None:
                            inverse_root(q)
                        if after:
                            after(ph, i, c)
                if peeled < ph.turns:
                    with act.Fori(peeled, ph.turns) as i:
                        for c in range(ph.body):
                            split_hi(ph, i, c)
                            if after:
                                after(ph, i, c)
                if end:
                    end()

            def into_stream(q):
                def after(ph, i, c):
                    if c % ph.per == ph.per - 1:
                        n = ph.out(i, c)
                        act.wait_ge(out_ready, n + 1)
                        stream(q, n - ph.out0, x)
                return after

            def ffn_split(p, h, f):
                act.wait_ge(prod_done, p + 1)
                A(tile(act_hi, f), two(prod, h), ACT.Copy).then_inc(ffn_hi, 1)

            def silu_gate(p, h, src):
                if not (type(p) is int and p < 2):
                    act.wait_ge(prod_done, p - 1)
                A(two(gate_s, h), src, ACT.Silu).then_inc(silu_done, 1)

            def swiglu(layer):
                def after(ph, i, c):
                    h = c // 2
                    p = FT * layer + 2 * i + h
                    if c % 2 == 0:
                        act.wait_ge(out_ready, ph.out(i, c) + 1)
                        silu_gate(p, h, two(gate, h))
                    else:
                        ffn_split(p, h, 2 * i + h)
                return after

            def last_tap(n, taps, j, n_conv, b):
                act.wait_ge(out_ready, n + 1)
                if not (type(n_conv) is int and n_conv < 2):
                    act.wait_ge(conv_b, n_conv - 1)
                wname, bname = ("conv4", "convb") if taps == 4 else ("conv3", "conv3b")
                A(two(tap_a, b), halo[:, b * 264 + 4:b * 264 + 260], ACT.Identity,
                  scale=pcol(wname, j * taps + taps - 1), bias=pcol(bname, j)).then_inc(conv_a, 1)

            def conv_swiglu(ph, i, c):
                j = 4 * i + c
                h = c // 2
                if c % 2 == 1:
                    p = 2 * FT + 2 * i + h
                    act.wait_ge(conv_d, 12 + j)
                    silu_gate(p, h, conv_out[:, 0:T])
                    if not (type(i) is int and i == 0 and h == 0):
                        ffn_split(p - 1, 1 - h, 2 * i + h - 1)
                last_tap(ph.out(i, c), 3, j, 12 + j, c % 2)

            def ssd_conv(t):
                if 1 <= t <= 12:
                    j = t - 1
                    act.wait_ge(conv_d, j + 1)
                    A(tile(u, 8 + j), two(conv_out, j % 2), ACT.Silu).then_inc(conv_silu, 1)
                if t < 12:
                    last_tap(PH["in2"].out0 + t, 4, t, t, t % 2)

            def squares(layer, t):
                n = norm_no(layer, t)
                arrived(act, layer, t + 1 if t < 64 and not (layer == 0 and t >= 37) else t)
                if n >= 2:
                    act.wait_ge(np_out, n - 1)
                a = t % 64
                A(normed(n), u[:, a * T:(a + 2) * T], ACT.Square).then_inc(np_sq, 1)

            def roots(n, width, scale, e):
                act.wait_ge(np_ms, n + 1)
                A(normed(n)[:, 0:width], bank[4][:, 0:width], ACT.Ln, scale=scale, bias=eps(e)).then_inc(np_ln, 1)
                act.wait_ge(np_ln, n + 1)
                A(normed(n)[:, 0:width], normed(n)[:, 0:width], ACT.Exp, scale=-0.5).then_inc(np_rt, 1)

            def norm(layer, t):
                _, scale, e, _, _ = SPEC[layer, t]
                roots(norm_no(layer, t), 512, scale, e)

            def group_norm(layer, g):
                n = number["norm", ("group_norm", layer, g)]
                act.wait_ge(np_out, n - 1)
                roots(n, T, 1.0, 0)

            def turn(layer, t):
                dst, c0 = TURN[layer, t]
                act.wait_ge(tr_ps, number["turn", (layer, t)] + 1)
                A(dst[:, :].rearrange("p (t c) -> p t c", t=2)[:, :, c0:c0 + P],
                  bank[5][:, 0:T].rearrange("p (t c) -> p t c", t=2), ACT.Copy).then_inc(tr_out, 1)

            def decays(layer, h):
                act.wait_ge(con_loaded, 16)
                A(u[:, DECAY + h * 384:DECAY + (h + 1) * 384], cmat("distT", 384), ACT.Exp, scale=LG[h]).then_inc(r_dec, 1)

            def ret_out(layer, h):
                act.wait_ge(r_o, h + 1)
                A(tile(u, 37 + h), bank[6][:, 0:T], ACT.Copy).then_inc(r_out, 1)

            def gate_silu(layer, n):
                arrived(act, 0, 13 + 2 * n)
                a = (12 + 2 * n) * T
                A(u[:, a:a + 2 * T], u[:, a:a + 2 * T], ACT.Silu).then_inc(r_gate, 1)

            def scores(layer, kind, h, m):
                n = number["scores", (layer, kind, h, m)]
                act.wait_ge(sm_m, n + 1)
                p = probs(n, layer)
                src = bank[2 + n % 2] if kind == "mem" else p
                if kind == "mem" and n >= 2:
                    act.wait_ge(sm_t, unit_head[n - 2] + 1)
                for it, (a, width) in enumerate([(0, T), (T, T)] if kind == "mem" else [(0, P), (P, T)]):
                    c = 2 * (n % 2) + it
                    last = A(p[:, a:a + width], src[:, a:a + width], ACT.Exp, bias=negmax[:, c:c + 1],
                             accum_out=rowsum[:, c:c + 1])
                last.then_inc(sm_e, 1)

            def weights(layer, kind, h):
                hd = number["weights", (layer, kind, h)]
                act.wait_ge(sm_t, hd + 1)
                if hd >= 2:
                    act.wait_ge(sm_o, hd - 1)
                width = 512 if kind == "mem" else 384
                A(probs_t(hd, layer)[:, 0:width], bank[5][:, 0:width], ACT.Copy).then_inc(sm_pt, 1)

            def mix(layer, k):
                t = mixed_tile(act, layer, k)
                A(tile(act_hi, k), tile(u, t), ACT.Copy).then_inc(mix_hi, 1)

            def c_times_b(layer, _):
                act.wait_ge(cb_ps, 2)
                for g in range(2):
                    A(cb[:, g * 384:(g + 1) * 384], bank[4 + g][:, 0:384], ACT.Copy).then_inc(cb_done, 1)

            def small_steps(layer, s):
                neg = small[:, T:2 * T]
                if s == 1:
                    act.wait_ge(dve_small, 3)
                    A(neg, neg, ACT.Exp).then_inc(act_small, 1)
                    act.wait_ge(act_small, 1)
                    A(neg, neg, ACT.Ln, bias=eps(3, 64)).then_inc(act_small, 1)
                    A(lam[0:64, 5:6], pcol("a_log", 0, 64), ACT.Exp).then_inc(act_small, 1)
                if s == 3:
                    act.wait_ge(pe_small, 1)
                    A(tmp[:, 0:1024].rearrange("p (k c) -> p k c", k=2)[:, :, 384:512],
                      bank[4][:, 0:256].rearrange("p (k c) -> p k c", k=2), ACT.Copy).then_inc(act_small, 1)

            def ssd_scores(layer, h):
                act.wait_ge(ss_b, h + 1)
                A(ssd_w(h), ssd_w(h), ACT.Exp).then_inc(ss_e, 1)

            def silu_z(layer, _):
                arrived(act, 2, 7)
                A(u[:, 0:8 * T], u[:, 0:8 * T], ACT.Silu).then_inc(z_silu, 1)

            def ssd_square(layer, t):
                act.wait_ge(ss_g, t + 1)
                if t:
                    act.wait_ge(gs_sum, t)
                if t == 4:
                    act.wait_ge(np_ms, number["norm", ("group_norm", 2, 0)] + 1)
                A(gsq if t % 4 else gsum, tile(u, 8 + t), ACT.Square).then_inc(gs_sq, 1)

            DO = {"squares": squares, "norm": norm, "group_norm": group_norm, "turn": turn, "decays": decays,
                  "ret_out": ret_out, "gate_silu": gate_silu, "scores": scores, "weights": weights, "mix": mix,
                  "cb": c_times_b, "small": small_steps, "ssd_scores": ssd_scores, "z_silu": silu_z,
                  "ssd_square": ssd_square}

            def follow(layer, slot0, before=None):
                def after(ph, i, c):
                    if before:
                        before(c)
                    for kind, *key in PLAN[layer][slot0 + c]:
                        if kind in DO:
                            DO[kind](layer, *key)
                return after

            act.wait_ge(par_loaded, 16)
            act.wait_ge(weighted, 10)
            for m in range(KT):
                act.wait_ge(mem_loaded[m // 4], 16)
                stream(0, m, u)
                if m == 4:
                    split_hi(PH["kv"], 0, -AHEAD)
            for g in range(1, AHEAD):
                split_hi(PH["kv"], 0, g - AHEAD)

            def kv_after(ph, i, c):
                if i == 0:
                    act.wait_ge(x_loaded, 16)
                    for m in (2 * c, 2 * c + 1):
                        stream(1, m, x)
            run("kv", kv_after, 0, unrolled=True)
            for layer in range(3):
                q = LAST_Q[layer]
                if layer == 1:
                    act.wait_ge(lam_ps, 1)
                    A(lam[:, 2:4], bank[5][:, 0:2], ACT.Exp, scale=1024.0).then_inc(lam_e, 1)
                run(f"in{layer}", follow(layer, 0, ssd_conv if layer == 2 else None), q)
                run(f"oa{layer}", follow(layer, PH[f"in{layer}"].n))
                run(f"ob{layer}", into_stream(q + 1), unrolled=True)
                if layer < 2:
                    run(f"up{layer}", swiglu(layer), q + 1)
                    run(f"down{layer}", into_stream(q + 2), unrolled=True)
            run("up2", conv_swiglu, 6, end=lambda: ffn_split(3 * FT - 1, 1, FT - 1))
            run("down2", None, unrolled=True)

        @block.gpsimd
        def _(pool):
            G = nc.gpsimd

            def squares(q, m):
                r = KT * q + m
                pool.wait_ge(sq_done, r + 1)
                if m == 0:
                    if q:
                        pool.wait_ge(ms_done, q)
                    G.tensor_copy(sqsum, two(sq, r % 2)).then_inc(ss_done, 1)
                else:
                    pool.wait_ge(ss_done, r)
                    G.tensor_tensor(sqsum, sqsum, two(sq, r % 2), ADD).then_inc(ss_done, 1)

            def lo(p, h, f):
                pool.wait_ge(ffn_hi, p + 1)
                G.tensor_tensor(tile(act_lo, f), two(prod, h), tile(act_hi, f).bitcast(f32), SUB).then_inc(ffn_lo, 1)

            def ffn(layer):
                with pool.Fori(0, FT // 2) as i:
                    for h in range(2):
                        lo(FT * layer + 2 * i + h, h, 2 * i + h)

            def conv_ffn():
                def product(i, h):
                    p = 2 * FT + 2 * i + h
                    pool.wait_ge(silu_done, p + 1)
                    pool.wait_ge(conv_d, 12 + 4 * i + 2 * h + 2)
                    if not (type(i) is int and i == 0):
                        pool.wait_ge(ffn_lo, p - 1)
                    G.tensor_tensor(two(prod, h), conv_out[:, T:2 * T], two(gate_s, h), MUL).then_inc(prod_done, 1)
                    lo(p, h, 2 * i + h)
                for h in range(2):
                    product(0, h)
                with pool.Fori(1, FT // 2) as i:
                    for h in range(2):
                        product(i, h)

            def mix(layer, k):
                pool.wait_ge(mix_hi, number["mix", (layer, k)] + 1)
                G.tensor_tensor(tile(act_lo, k), tile(u, mixed_tile(None, layer, k)),
                                tile(act_hi, k).bitcast(f32), SUB).then_inc(mix_lo, 1)

            def ssd_square(layer, t):
                pool.wait_ge(gs_sq, t + 1)
                if t % 4 == 0:
                    pool.nop().then_inc(gs_sum, 1)
                else:
                    pool.wait_ge(gs_sum, t)
                    G.tensor_tensor(gsum, gsum, gsq, ADD).then_inc(gs_sum, 1)

            for q in (0, 1):
                for m in range(KT):
                    squares(q, m)
            for layer in range(3):
                for steps in PLAN[layer]:
                    for kind, *key in steps:
                        if kind == "mix":
                            mix(layer, *key)
                        if kind == "ssd_square":
                            ssd_square(layer, *key)
                for m in range(KT):
                    squares(2 + 2 * layer, m)
                if layer == 2:
                    conv_ffn()
                    break
                ffn(layer)
                for m in range(KT):
                    squares(3 + 2 * layer, m)

        @block.vector
        def _(dve):
            V = nc.vector

            def split_lo(ph, i, c):
                g0 = ph.ring0 + c + AHEAD
                slot, g = g0 % RING, g0 + ph.body * i
                known = type(i) is int
                if known:
                    if g >= NRING:
                        return
                    slot = g % RING
                width = WIDTH[g] if known else DM
                dve.wait_ge(hi_done, g + 1)
                a, b = slot * DM, slot * DM + width
                V.tensor_tensor(ring_lo[:, a:b], ring_raw[:, a:b], ring_hi[:, a:b].bitcast(f32), SUB).then_inc(lo_done, 1)

            def stream_lo(q, m, src):
                name, _, hi, lo = NORMS[q]
                dve.wait_ge(xh_done, KT * q + m + 1)
                V.scalar_tensor_tensor(tile(lo, m), tile(src, m), pcol(name, m), tile(hi, m).bitcast(f32),
                                       MUL, SUB).then_inc(xl_done, 1)

            def refine(q):
                dve.wait_ge(root_done, q + 1)
                v = bank[7][:, 0:T]
                V.scalar_tensor_tensor(v, v, eps(0), rstd[:, :], ADD, MUL).then_inc(newton, 1)
                dve.wait_ge(newton, 2 * q + 1)
                V.tensor_tensor(v, v, rstd[:, :], MUL).then_inc(newton, 1)
                dve.wait_ge(newton, 2 * q + 2)
                V.scalar_tensor_tensor(rstd[:, :], v, -3.0, rstd[:, :], ADD, MUL).then_inc(rstd_done, 1)
                dve.wait_ge(rstd_done, q + 1)

            def run(name, evac, after=None, q=None, unrolled=False, before=None, before_split=None, end=None):
                ph = PH[name]
                peeled = ph.turns if unrolled else 1

                def step(i, c):
                    if before:
                        before(ph, i, c)
                    if c % ph.per == ph.per - 1:
                        if type(i) is int and i == 0 and c == 0 and q is not None:
                            refine(q)
                        dve.wait_ge(tile_done, ph.tile(i, c)[1] + 1)
                        evac(ph, i, c, bank[(ph.out0 + c // ph.per + (ph.body // ph.per * i if type(i) is int else 0)) % 2][:, 0:T])
                    if before_split:
                        before_split(ph, i, c)
                    split_lo(ph, i, c)
                    if after:
                        after(ph, i, c)
                for i in range(peeled):
                    for c in range(ph.body):
                        step(i, c)
                if peeled < ph.turns:
                    with dve.Fori(peeled, ph.turns) as i:
                        for c in range(ph.body):
                            step(i, c)
                if end:
                    end()

            def kv_evac(ph, i, c, ps):
                V.tensor_tensor(tile(u, 20 + ph.out(i, c) - ph.out0), ps, rstd[:, :], MUL).then_inc(out_ready, 1)

            def add_to_x(ph, i, c, ps):
                m = ph.out(i, c) - ph.out0
                V.tensor_tensor(tile(x, m), tile(x, m), ps, ADD).then_inc(out_ready, 1)

            def into_stream(q):
                def after(ph, i, c):
                    if c % ph.per == ph.per - 1:
                        stream_lo(q, ph.out(i, c) - ph.out0, x)
                return after

            def swiglu_evac(layer):
                def evac(ph, i, c, ps):
                    h = c // 2
                    if c % 2 == 1 and not (layer == 0 and type(i) is int):
                        dve.wait_ge(prod_done, FT * layer + 2 * i + h - 1)
                    V.tensor_tensor(two(val if c % 2 else gate, h), ps, rstd[:, :], MUL).then_inc(out_ready, 1)
                return evac

            def swiglu_after(layer):
                def after(ph, i, c):
                    if c % 2 == 1:
                        h = c // 2
                        p = FT * layer + 2 * i + h
                        dve.wait_ge(out_ready, ph.out(i, c) + 1)
                        dve.wait_ge(silu_done, p + 1)
                        if not (type(p) is int and p < 2):
                            dve.wait_ge(ffn_lo, p - 1)
                        V.tensor_tensor(two(prod, h), two(val, h), two(gate_s, h), MUL).then_inc(prod_done, 1)
                return after

            def halo_evac(ph, i, c, ps):
                b = c % 2
                V.tensor_tensor(halo[:, b * 264 + 4:b * 264 + 260], ps, rstd[:, :], MUL).then_inc(out_ready, 1)

            def other_taps(wname, taps, j, n_conv, b, into):
                dve.wait_ge(conv_a, n_conv + 1)
                chain = {4: [(conv_b, two(tap_b, b)), (conv_c, two(tap_c, b)), (conv_d, into)],
                         3: [(conv_b, two(tap_b, b)), (conv_d, into)]}[taps]
                acc = two(tap_a, b)
                for s, (done, dst) in enumerate(chain):
                    V.scalar_tensor_tensor(dst, halo[:, b * 264 + 3 - s:b * 264 + 259 - s],
                                           pcol(wname, j * taps + taps - 2 - s), acc, MUL, ADD).then_inc(done, 1)
                    dve.wait_ge(done, n_conv + 1)
                    acc = dst

            def conv_before(ph, i, c):
                if type(i) is int and i == 0 and c == 0:
                    return
                b = (c - 1) % 2
                j = 4 * i + c - 1
                if b == 0:
                    if not (type(i) is int and i == 0 and c == 1):
                        dve.wait_ge(silu_done, 2 * FT + 2 * i + c // 2)
                elif not (type(i) is int and i == 0 and c < 3):
                    dve.wait_ge(prod_done, 2 * FT + 2 * i + c // 2 - 1)
                other_taps("conv3", 3, j, 12 + j, b, two(conv_out, b))

            def conv_end():
                dve.wait_ge(prod_done, 3 * FT - 1)
                other_taps("conv3", 3, 43, 55, 1, two(conv_out, 1))

            def in_evac(layer):
                def evac(ph, i, c, ps):
                    t = ORDER[ph.name][c]
                    if t == SMALL:
                        dve.wait_ge(ss_done, 6 * KT)
                        dve.wait_ge(rstd_done, 6)
                        V.memset(small, 0.0).then_inc(small_zero, 1)
                        dve.wait_ge(small_zero, 1)
                        V.tensor_tensor(small[:, 0:T], ps[0:64, :], rstd[0:64, :], MUL).then_inc(out_ready, 1)
                    elif layer == 2 and c < 12:
                        halo_evac(ph, i, c, ps)
                    else:
                        V.tensor_tensor(tile(u, t), ps, rstd[:, :], MUL).then_inc(out_ready, 1)
                return evac

            def ssd_conv(ph, i, t):
                if type(t) is int and 1 <= t <= 12:
                    j = t - 1
                    if j >= 2:
                        dve.wait_ge(conv_silu, j - 1)
                    other_taps("conv4", 4, j, j, j % 2, two(conv_out, j % 2))

            def newton_step(n, width):
                dve.wait_ge(np_rt, n + 1)
                v, y = bank[4][:, 0:width], normed(n)[:, 0:width]
                V.scalar_tensor_tensor(v, v, eps(0), y, ADD, MUL).then_inc(np_nt, 1)
                dve.wait_ge(np_nt, 3 * n + 1)
                V.tensor_tensor(v, v, y, MUL).then_inc(np_nt, 1)
                dve.wait_ge(np_nt, 3 * n + 2)
                return v, y

            def norm_out(layer, t):
                n = norm_no(layer, t)
                _, scale, _, name, k = SPEC[layer, t]
                v, y = newton_step(n, 512)
                V.scalar_tensor_tensor(y, v, -3.0 / scale, y, ADD, MUL).then_inc(np_nt, 1)
                dve.wait_ge(np_nt, 3 * n + 3)
                a = t % 64
                if name == "gn":
                    for s in range(2):
                        last = V.scalar_tensor_tensor(tile(u, a + s), tile(u, a + s), pcol(name, k + s),
                                                      two(normed(n), s), MUL, MUL)
                else:
                    last = V.scalar_tensor_tensor(u[:, a * T:(a + 2) * T], u[:, a * T:(a + 2) * T], pcol(name, k),
                                                  normed(n), MUL, MUL)
                last.then_inc(np_out, 1)

            def group_out(layer, g):
                n = number["norm", ("group_norm", layer, g)]
                v, y = newton_step(n, T)
                V.scalar_tensor_tensor(y, v, -3.0, y, ADD, MUL).then_inc(np_nt, 1)
                dve.wait_ge(np_nt, 3 * n + 3)
                for t in range(4 * g, 4 * g + 4):
                    y = tile(u, 8 + t)
                    last = V.scalar_tensor_tensor(y, y, pcol("ssdn", t), normed(n)[:, 0:T], MUL, MUL)
                last.then_inc(np_out, 1)

            def ret_scores(layer, h):
                dve.wait_ge(r_s, h + 1)
                dve.wait_ge(r_dec, h + 1)
                if h:
                    dve.wait_ge(r_o, h)
                V.scalar_tensor_tensor(decayed, bank[7][:, 0:384], 64.0 ** -0.5,
                                       u[:, DECAY + h * 384:DECAY + (h + 1) * 384], MUL, MUL).then_inc(r_pt, 1)

            def gated(layer, n):
                dve.wait_ge(r_gate, n + 1)
                dve.wait_ge(np_out, norm_no(0, 37 + 2 * n) + 1)
                a, g = 37 + 2 * n, 12 + 2 * n
                V.tensor_tensor(u[:, a * T:(a + 2) * T], u[:, a * T:(a + 2) * T], u[:, g * T:(g + 2) * T],
                                MUL).then_inc(r_gated, 1)

            def scores(layer, kind, h, m):
                n = number["scores", (layer, kind, h, m)]
                dve.wait_ge(sm_s, n + 1)
                b, c = bank[2 if layer == 2 else 2 + n % 2], 2 * (n % 2)
                if kind == "mem":
                    V.tensor_reduce(negmax[:, c:c + 2], b[:, :].rearrange("p (t c) -> p t c", t=2), AX, ALU.max,
                                    negate=True).then_inc(sm_m, 1)
                    return
                s = probs(n, layer)
                if unit_ends[n - 2]:
                    dve.wait_ge(sm_t, unit_head[n - 2] + 1)
                else:
                    dve.wait_ge(sm_n, unit_head[n - 2] + 1)
                if kind == "diff":
                    V.scalar_tensor_tensor(s[:, 0:384], cmat("dist", 384), -SLOPE[h], b[:, 0:384], MUL, ADD).then_inc(sm_b, 2)
                else:
                    for it, (a, width) in enumerate([(0, P), (P, T)]):
                        mask = con[:, CCOL["causal"] + a:CCOL["causal"] + a + width]
                        k = it * 64 + 32 + h
                        V.scalar_tensor_tensor(s[:, a:a + width], b[:, a:a + width], small_tok(k), mask,
                                               ADD, ADD).then_inc(sm_b, 1)
                dve.wait_ge(sm_b, 2 * number["biased", (layer, kind, h, m)] + 2)
                for it, (a, width) in enumerate([(0, P), (P, T)]):
                    last = V.tensor_reduce(negmax[:, c + it:c + it + 1], s[:, a:a + width], AX, ALU.max, negate=True)
                last.then_inc(sm_m, 1)

            sm_r_count = [0]

            def small_op(*ins):
                for x_ in ins:
                    x_.then_inc(sm_r, 1)
                sm_r_count[0] += len(ins)
                dve.wait_ge(sm_r, sm_r_count[0])

            def softmax(layer, kind, h, m):
                n = number["scores", (layer, kind, h, m)]
                dve.wait_ge(sm_e, n + 1)
                c = 2 * (n % 2)
                small_op(V.reciprocal(rrow[:, c:c + 2], rowsum[:, c:c + 2]))
                p = probs(n, layer)
                if kind != "diff":
                    for it, (a, width) in enumerate([(0, T), (T, T)] if kind == "mem" else [(0, P), (P, T)]):
                        last = V.tensor_scalar(p[:, a:a + width], p[:, a:a + width], rrow[:, c + it:c + it + 1], None, MUL)
                    last.then_inc(sm_n, 1)
                elif m == 1:
                    small_op(V.tensor_scalar(rrow[:, c:c + 2], rrow[:, c:c + 2], lam[:, 4:5], None, MUL))
                    small_op(*[V.tensor_scalar(p[:, a:a + width], p[:, a:a + width], rrow[:, c + it:c + it + 1], None, MUL)
                               for it, (a, width) in enumerate([(0, P), (P, T)])])
                    first, c0 = probs(n - 1, layer), 2 * ((n - 1) % 2)
                    for it, (a, width) in enumerate([(0, P), (P, T)]):
                        last = V.scalar_tensor_tensor(p[:, a:a + width], first[:, a:a + width],
                                                      rrow[:, c0 + it:c0 + it + 1], p[:, a:a + width], MUL, ADD)
                    last.then_inc(sm_n, 1)

            def values(layer, kind, h):
                t, full = filled(layer, kind, h)
                if full:
                    dve.wait_ge(sm_o, number["weights", (layer, kind, h)] + 1)
                    V.tensor_copy(tile(u, t), bank[6][:, 0:T]).then_inc(sm_out, 1)

            def small_steps(layer, s):
                z, neg, dt, lg = (small[:, k * T:(k + 1) * T] for k in range(4))
                if s == 0:
                    dve.wait_ge(out_ready, PH["in2"].out0 + 13)
                    V.tensor_scalar(z, z, pcol("small_b", 0, 64), None, ADD).then_inc(dve_small, 1)
                    dve.wait_ge(dve_small, 1)
                    V.scalar_tensor_tensor(neg, z, -1.0, z, MUL, ALU.min).then_inc(dve_small, 2)
                if s == 2:
                    dve.wait_ge(act_small, 3)
                    V.scalar_tensor_tensor(dt[0:16], z[0:16], 0.0, neg[0:16], ALU.max, ADD).then_inc(dve_small, 1)
                    V.scalar_tensor_tensor(lg[32:64], z[32:64], 0.0, neg[32:64], ALU.min, SUB).then_inc(dve_small, 1)
                    dve.wait_ge(dve_small, 5)
                    V.tensor_scalar(lg[0:16], dt[0:16], lam[0:16, 5:6], -1.0, MUL, MUL).then_inc(dve_small, 1)
                    V.memset(neg, 1.0).then_inc(dve_small, 1)
                    dve.wait_ge(dve_small, 7)
                    V.tensor_tensor_scan(z, neg, lg, 0.0, MUL, ADD).then_inc(dve_small, 1)
                    dve.wait_ge(dve_small, 8)
                    V.tensor_scalar(neg, z, -1.0, None, MUL).then_inc(dve_small, 1)

            def ssd_scores(layer, h):
                s = ssd_w(h)
                if h == 0:
                    dve.wait_ge(act_small, 4)
                    dve.wait_ge(cb_done, 2)
                dve.wait_ge(ss_bc, h + 1)
                if h >= 2:
                    dve.wait_ge(ss_y, h - 1)
                for st, (a, q0, width) in enumerate([(0, 0, T), (T, P, P)]):
                    k = st * 64 + h
                    last = V.scalar_tensor_tensor(s[:, a:a + width], bank[3][:, q0:q0 + width], small_tok(k),
                                                  con[:, CCOL["causalT"] + a:CCOL["causalT"] + a + width], SUB, ADD)
                last.then_inc(ss_b, 1)

            def ssd_weights(layer, h):
                s = ssd_w(h)
                dve.wait_ge(ss_e, h + 1)
                g = h // 8
                for st, (a, width) in enumerate([(0, T), (T, P)]):
                    k = P + st * 64 + h
                    last = V.scalar_tensor_tensor(s[:, a:a + width], s[:, a:a + width],
                                                  small_tok(k), cb[:, g * 384 + a:g * 384 + a + width], MUL, MUL)
                last.then_inc(ss_p, 1)

            def ssd_out(layer, h):
                if h % 2 == 0:
                    return
                t = h // 2
                dve.wait_ge(ss_y, 2 * t + 2)
                y = tile(u, 8 + t)
                V.scalar_tensor_tensor(y, y, pcol("skip", t), bank[7][:, 0:T], MUL, ADD).then_inc(ss_s, 1)

            def ssd_gate(layer, t):
                dve.wait_ge(ss_s, t + 1)
                dve.wait_ge(z_silu, 1)
                y = tile(u, 8 + t)
                V.tensor_tensor(y, y, tile(u, t), MUL).then_inc(ss_g, 1)

            DO = {"norm_out": norm_out, "norm_soon": norm_out, "group_out": group_out, "ret_scores": ret_scores, "gated": gated, "scores": scores,
                  "softmax": softmax, "values": values, "small": small_steps, "ssd_scores": ssd_scores,
                  "ssd_weights": ssd_weights, "ssd_out": ssd_out, "ssd_gate": ssd_gate}

            def follow(layer, slot0, kinds):
                def steps(ph, i, c):
                    for kind, *key in PLAN[layer][slot0 + c]:
                        if kind in kinds:
                            DO[kind](layer, *key)
                return steps

            EARLY = {"norm_out", "softmax", "ssd_weights"}
            MIDDLE = {"norm_soon", "group_out"}
            LATE = set(DO) - EARLY - MIDDLE

            V.memset(halo[:, :], 0.0).then_inc(halo_zero, 1)
            dve.wait_ge(par_loaded, 16)
            carried = [("memq0", 2, 64.0), ("memk0", 2, 1.0), ("gn", 6, 1.0), ("diffq", 1, 64.0), ("diffk", 1, 1.0),
                       ("subln", 1, OUT), ("ssdn", 8, 1.0), ("foxq", 1, 64.0), ("foxk", 1, 1.0)]
            for name, width, s_ in carried:
                cols = par[:, PCOL[name]:PCOL[name] + width]
                V.tensor_scalar(cols, cols, -0.5 * s_, None, MUL).then_inc(weighted, 1)
            residual = par[:, PCOL["attn0"]:PCOL["memq0"]]
            V.tensor_scalar(residual, residual, -0.5, None, MUL).then_inc(weighted, 1)
            dve.wait_ge(weighted, len(carried) + 1)
            for m in range(KT):
                stream_lo(0, m, u)
                if m == 4:
                    split_lo(PH["kv"], 0, -AHEAD)
            for g in range(1, AHEAD):
                split_lo(PH["kv"], 0, g - AHEAD)

            def kv_after(ph, i, c):
                if i == 0:
                    for m in (2 * c, 2 * c + 1):
                        stream_lo(1, m, x)
            run("kv", kv_evac, kv_after, 0, unrolled=True)
            lc = PCOL["lam"]
            for s in range(2):
                last = V.tensor_tensor(lam[0:64, s:s + 1], par[0:64, lc + 2 * s:lc + 2 * s + 1],
                                       par[0:64, lc + 2 * s + 1:lc + 2 * s + 2], MUL)
            last.then_inc(lam_in, 1)
            dve.wait_ge(halo_zero, 1)
            dve.wait_ge(con_loaded, 16)
            for layer in range(3):
                q = LAST_Q[layer]
                if layer == 1:
                    dve.wait_ge(lam_e, 1)
                    V.tensor_scalar(lam[:, 4:5], lam[:, 3:4], lam[:, 2:3], LAMBDA_INIT, SUB, SUB).then_inc(lam_done, 1)
                    dve.wait_ge(lam_done, 1)

                def middle(ph, i, c):
                    if layer == 2:
                        ssd_conv(ph, i, c)
                    follow(layer, 0, MIDDLE)(ph, i, c)
                n_in = PH[f"in{layer}"].n
                run(f"in{layer}", in_evac(layer), follow(layer, 0, LATE), q, before=follow(layer, 0, EARLY),
                    before_split=middle)
                run(f"oa{layer}", add_to_x, follow(layer, n_in, LATE), before=follow(layer, n_in, EARLY),
                    before_split=follow(layer, n_in, MIDDLE))
                run(f"ob{layer}", add_to_x, into_stream(q + 1), unrolled=True)
                if layer < 2:
                    run(f"up{layer}", swiglu_evac(layer), swiglu_after(layer), q + 1)
                    run(f"down{layer}", add_to_x, into_stream(q + 2), unrolled=True)
            run("up2", halo_evac, None, 6, before_split=conv_before, end=conv_end)
            run("down2", add_to_x, None, unrolled=True)


def column_tiles(a):
    k, n = a.shape
    return np.ascontiguousarray(a.reshape(k // P, P, n // P, P).transpose(2, 1, 0, 3).reshape(n, k))


def features(a):
    return a.reshape(-1, P).T


def kernel(**inputs):
    import concourse.bacc as bacc
    from concourse.bass_utils import run_bass_kernel_spmd

    a = {k: np.ascontiguousarray(v) for k, v in inputs.items()}
    w = {}
    w["kv"] = np.concatenate([column_tiles(a["w_mem_kv"][l]) for l in range(2)])

    def interleaved(m, n):
        return column_tiles(m).reshape(2, n, P, -1).transpose(1, 0, 2, 3).reshape(2 * n * P, -1)
    def rows(m, name):
        return np.concatenate([m[k * P:(k + 1) * P] for k in OUT_INPUTS[name]])

    def in_order(m, name):
        return column_tiles(np.concatenate([m[:, t * P:(t + 1) * P] for t in ORDER[name]], 1))
    w_in2 = a["w_in_2"][0]
    small = np.zeros((DM, P), np.float32)
    small[:, 0:16] = w_in2[:, 2560:2576]
    small[:, 32:48] = w_in2[:, 5648:5664]
    w_in2 = np.concatenate([w_in2[:, 0:2560], w_in2[:, 2576:5648], small], 1)
    for l, (w_in, w_out, w_up, w_down) in enumerate([
            (a["w_in"][0], a["w_out"][0], a["w_gate_up"][0], a["w_down"][0]),
            (a["w_in"][1], a["w_out"][1], a["w_gate_up"][1], a["w_down"][1]),
            (w_in2, a["w_out_2"][0], a["w_up_2"][0], a["w_down_2"][0])]):
        w[f"in{l}"] = in_order(w_in, f"in{l}")
        w[f"oa{l}"] = column_tiles(rows(w_out, f"oa{l}"))
        w[f"ob{l}"] = column_tiles(rows(w_out, f"ob{l}"))
        w[f"up{l}"] = interleaved(w_up, FT)
        w[f"down{l}"] = column_tiles(w_down)

    par = np.zeros((P, NPARAM), np.float32)

    def put(name, v):
        par[0:v.shape[0], PCOL[name]:PCOL[name] + v.shape[1]] = v

    def twice(v):
        return np.concatenate([v, v]).reshape(P, 1)
    for l in range(2):
        put(f"attn{l}", features(a["attn_norm_w"][l]))
        put(f"ffn{l}", features(a["ffn_norm_w"][l]))
        put(f"memq{l}", twice(a["mem_q_norm_w"][l]))
        put(f"memk{l}", twice(a["mem_k_norm_w"][l]))
    put("mem", features(a["mem_norm_w"]))
    put("mix2", features(a["norm_mix_w_2"][0]))
    put("ffn2", features(a["norm_ffn_w_2"][0]))
    put("gn", features(a["ret_gn_w"][0]))
    put("diffq", twice(a["diff_q_norm_w"][0]))
    put("diffk", twice(a["diff_k_norm_w"][0]))
    put("subln", features(a["diff_subln_w"][0]))
    put("lam", np.stack([a[f"diff_lambda_{n}"][0] for n in ("q1", "k1", "q2", "k2")], 1))
    put("conv4", a["ssd_conv_w_2"][0].reshape(4, 12, P).transpose(2, 1, 0).reshape(P, 48))
    put("convb", features(a["ssd_conv_b_2"][0]))
    bias = np.zeros((64, 1), np.float32)
    bias[0:16, 0] = a["ssd_dt_bias_2"][0]
    bias[32:48, 0] = a["fox_f_bias_2"][0]
    put("small_b", bias)
    put("a_log", a["ssd_a_log_2"][0].reshape(16, 1))
    put("skip", features(np.repeat(a["ssd_d_2"][0], 64)))
    put("ssdn", features(a["ssd_norm_w_2"][0]))
    put("foxq", twice(a["fox_q_norm_w_2"][0]))
    put("foxk", twice(a["fox_k_norm_w_2"][0]))
    put("conv3", a["ffn_conv_w_2"][0].reshape(3, 2, FT, P).transpose(3, 2, 1, 0).reshape(P, 132))
    put("eps", np.tile(np.array([[EPS, 64 * EPS, EPS / (1 - LAMBDA_INIT) ** 2, 1.0]], np.float32), (P, 1)))
    put("conv3b", a["ffn_conv_b_2"][0].reshape(2, FT, P).transpose(2, 1, 0).reshape(P, 44))

    def feature_major(m):
        return np.ascontiguousarray(m.reshape(T, KT, P).transpose(2, 1, 0).reshape(P, KT * T))

    arrays = {"x_in": feature_major(a["x"]), "mem_in": feature_major(a["mem"]), "params_in": par,
              "consts_in": constants()}
    arrays.update({f"w_{n}": np.ascontiguousarray(m) for n, m in w.items()})
    nc = bacc.Bacc("TRN2", target_bir_lowering=False, num_devices=1)
    ap = {n: nc.dram_tensor(n, list(m.shape), mybir.dt.float32, kind="ExternalInput").ap() for n, m in arrays.items()}
    out = nc.dram_tensor("out", [P, KT * T], mybir.dt.float32, kind="ExternalOutput").ap()
    program(nc, ap["x_in"], ap["mem_in"], ap["params_in"], ap["consts_in"], {n: ap[f"w_{n}"] for n in w}, out)
    r = run_bass_kernel_spmd(nc, [arrays], core_ids=[0])
    y = r.results[0]["out"]
    return y.reshape(P, KT, T).transpose(2, 1, 0).reshape(1, T, DM)
```
